# Optimizing a Trainium2 kernel written in Bass

```python
import jax
import jax.numpy as jnp
from jax import lax
import numpy as np

D_MODEL = 1024
BATCH = 1
SEQ = 256
DEPTH = 2

GRID_W = 64
CTX_LEN = 256
EPS = 1e-6

POOL_WIDTH = 512
POOL_WINDOWS = (2, 4, 8, 16)
POOL_GROUP = POOL_WIDTH // len(POOL_WINDOWS)

HY_WIDTH = 512
HY_EMB = 33
HY_BANDS = (HY_EMB - 1) // 2
HY_FILTER_HIDDEN = 64

MLA_HEADS = 8
QK_NOPE = 64
QK_ROPE = 32
QK_DIM = QK_NOPE + QK_ROPE
V_HEAD = 64
Q_LORA = 384
KV_LORA = 256
MLA_SCALE = QK_DIM ** -0.5
ROPE_BASE = 10000.0
Q_BLOCK = 128

D_FF = 4 * D_MODEL
N_BRANCH = 3
N_MOD = 6

OFF_POOL = 0
OFF_HY = OFF_POOL + POOL_WIDTH
OFF_Q = OFF_HY + 3 * HY_WIDTH
OFF_KV = OFF_Q + Q_LORA
OFF_GATE = OFF_KV + KV_LORA + QK_ROPE
D_IN = OFF_GATE + N_BRANCH * D_MODEL

kernel_name = 'hybrid_pool_hyena_mla_prefix_dit'

def rmsnorm(x, g):
    xf = x.astype(jnp.float32)
    y = xf * lax.rsqrt(jnp.mean(xf * xf, axis=-1, keepdims=True) + EPS)
    return (y * g.astype(jnp.float32)).astype(x.dtype)

def axial_rope_tables(n_rows):
    f32 = jnp.float32
    rows = jnp.repeat(jnp.arange(n_rows, dtype=f32), GRID_W)
    cols = jnp.tile(jnp.arange(GRID_W, dtype=f32), n_rows)
    half = QK_ROPE // 2
    inv = ROPE_BASE ** (-jnp.arange(0, half, 2, dtype=f32) / half)
    ar = rows[:, None] * inv
    ac = cols[:, None] * inv
    ang = jnp.concatenate([ar, ar, ac, ac], axis=-1)
    return jnp.cos(ang), jnp.sin(ang)

def apply_axial_rope(x, cos, sin):
    q = QK_ROPE // 4
    rot = jnp.concatenate([-x[..., q:2 * q], x[..., :q], -x[..., 3 * q:], x[..., 2 * q:3 * q]], axis=-1)
    return x * cos.astype(x.dtype) + rot * sin.astype(x.dtype)

def pool_mixer(p, w_group, scale):
    f32 = jnp.float32
    b_, L, _ = p.shape
    pf = p.astype(f32)
    cs = jnp.concatenate([jnp.zeros((b_, 1, POOL_WIDTH), f32), jnp.cumsum(pf, axis=1)], axis=1)
    t = jnp.arange(L)
    outs = []
    for gi, w in enumerate(POOL_WINDOWS):
        lo = jnp.clip(t - w // 2, 0, L)
        hi = jnp.clip(t + w // 2, 0, L)
        sl = slice(gi * POOL_GROUP, (gi + 1) * POOL_GROUP)
        csg = cs[:, :, sl]
        mean = (jnp.take(csg, hi, axis=1) - jnp.take(csg, lo, axis=1)) / (hi - lo).astype(f32)[None, :, None]
        outs.append(mean - pf[:, :, sl])
    u = jnp.stack(outs, axis=2).astype(p.dtype)
    u = jnp.einsum('blgc,gcd->blgd', u, w_group).reshape(b_, L, POOL_WIDTH)
    return u * scale

def short_conv(u, w, b):
    up = jnp.pad(u, ((0, 0), (1, 1), (0, 0)))
    return up[:, :-2] * w[0] + up[:, 1:-1] * w[1] + up[:, 2:] * w[2] + b

def hyena_filter(L, w1, b1, freq1, w2, b2, freq2, w3, decay):
    f32 = jnp.float32
    t = jnp.linspace(0.0, 1.0, L, dtype=f32)[:, None]
    omega = 2.0 * np.pi * jnp.arange(L, dtype=f32)[:, None] / L
    bands = jnp.linspace(1e-4, HY_BANDS - 1, HY_BANDS, dtype=f32)[None, :]
    z = jnp.concatenate([t, jnp.cos(omega * bands), -jnp.sin(omega * bands)], axis=-1)
    hid = jnp.sin(freq1.astype(f32) * (z @ w1.astype(f32) + b1.astype(f32)))
    hid = jnp.sin(freq2.astype(f32) * (hid @ w2.astype(f32) + b2.astype(f32)))
    h = (hid @ w3.astype(f32)).reshape(L, 2, HY_WIDTH)
    h = h * jnp.exp(-t[:, :, None] * jnp.abs(decay.astype(f32)))
    h_fwd, h_bwd = h[:, 0], h[1:, 1]
    l1 = jnp.sum(jnp.abs(h_fwd), axis=0) + jnp.sum(jnp.abs(h_bwd), axis=0)
    filt = jnp.concatenate([h_fwd, jnp.zeros((1, HY_WIDTH), f32), h_bwd[::-1]], axis=0)
    return filt / l1

def long_conv(u, filt):
    L = u.shape[1]
    u_f = jnp.fft.rfft(u.astype(jnp.float32), n=2 * L, axis=1)
    f_f = jnp.fft.rfft(filt, n=2 * L, axis=0)
    y = jnp.fft.irfft(u_f * f_f[None], n=2 * L, axis=1)[:, :L]
    return y.astype(u.dtype)

def hyena_mixer(u, lp):
    L = u.shape[1]
    x0, x1, v = jnp.split(short_conv(u, lp['hy_conv_w'], lp['hy_conv_b']), 3, axis=-1)
    filt = hyena_filter(L, lp['hy_f_w1'], lp['hy_f_b1'], lp['hy_f_freq1'], lp['hy_f_w2'],
                        lp['hy_f_b2'], lp['hy_f_freq2'], lp['hy_f_w3'], lp['hy_decay'])
    zv = v * x1
    return x0 * (long_conv(zv, filt) + zv * lp['hy_bias'])

def mla_query(c_q, q_norm_g, w_uq, cos, sin):
    b_, L, _ = c_q.shape
    q = (rmsnorm(c_q, q_norm_g) @ w_uq).reshape(b_, L, MLA_HEADS, QK_DIM)
    if cos is None:
        return q
    q_pe = apply_axial_rope(q[..., QK_NOPE:], cos[None, :, None, :], sin[None, :, None, :])
    return jnp.concatenate([q[..., :QK_NOPE], q_pe], axis=-1)

def mla_kv(c_kv, kv_norm_g, w_ukv, cos, sin):
    b_, L, _ = c_kv.shape
    kv = (rmsnorm(c_kv[..., :KV_LORA], kv_norm_g) @ w_ukv).reshape(b_, L, MLA_HEADS, QK_NOPE + V_HEAD)
    k_nope, v = kv[..., :QK_NOPE], kv[..., QK_NOPE:]
    k_pe = c_kv[..., KV_LORA:]
    if cos is not None:
        k_pe = apply_axial_rope(k_pe, cos[None], sin[None])
    k_pe = jnp.broadcast_to(k_pe[:, :, None, :], (b_, L, MLA_HEADS, QK_ROPE))
    return jnp.concatenate([k_nope, k_pe], axis=-1), v

def attend(q, k, v):
    s = jnp.einsum('bqhd,bkhd->bhqk', q, k).astype(jnp.float32) * MLA_SCALE
    p = jax.nn.softmax(s, axis=-1).astype(v.dtype)
    return jnp.einsum('bhqk,bkhd->bqhd', p, v)

def blocked_attend(q, k, v):
    b_, L, H, dk = q.shape
    qb = q.reshape(b_, L // Q_BLOCK, Q_BLOCK, H, dk).transpose(1, 0, 2, 3, 4)
    ob = lax.map(lambda qi: attend(qi, k, v), qb)
    return ob.transpose(1, 0, 2, 3, 4).reshape(b_, L, H, V_HEAD)

def token_mix(proj, k_ctx, v_ctx, lp, cos, sin):
    b_, L, _ = proj.shape
    ga, gb, gc = jnp.split(jax.nn.sigmoid(proj[..., OFF_GATE:]), N_BRANCH, axis=-1)
    a = pool_mixer(proj[..., OFF_POOL:OFF_HY], lp['pool_w'], lp['pool_scale']) @ lp['pool_out']
    b = hyena_mixer(proj[..., OFF_HY:OFF_Q], lp) @ lp['hy_out']
    q = mla_query(proj[..., OFF_Q:OFF_KV], lp['q_norm_g'], lp['w_uq'], cos, sin)
    if cos is None:
        o = attend(q, k_ctx, v_ctx)
    else:
        k_lat, v_lat = mla_kv(proj[..., OFF_KV:OFF_GATE], lp['kv_norm_g'], lp['w_ukv'], cos, sin)
        o = blocked_attend(q, jnp.concatenate([k_ctx, k_lat], axis=1), jnp.concatenate([v_ctx, v_lat], axis=1))
    cm = o.reshape(b_, L, MLA_HEADS * V_HEAD) @ lp['w_o']
    return (ga * a + gb * b + gc * cm) @ lp['w_out']

def sq_relu_mlp(x, w1, w2):
    return jnp.square(jax.nn.relu(x @ w1)) @ w2

def setup_inputs(seed: int = 0) -> dict:
    key = jax.random.key(seed)
    ks = iter(jax.random.split(key, 40))
    f32 = jnp.float32

    def nrm(shape, s):
        return jax.random.normal(next(ks), shape, f32) * s

    def gain(shape):
        return 1.0 + nrm(shape, 0.02)

    L_ = DEPTH
    return {
        'x': nrm((BATCH, SEQ, D_MODEL), 1.0),
        'c': nrm((BATCH, D_MODEL), 1.0),
        'ctx': nrm((BATCH, CTX_LEN, D_MODEL), 1.0),
        'c_ctx': nrm((D_MODEL,), 1.0),
        'w_mod': nrm((L_, D_MODEL, N_MOD * D_MODEL), 0.5 * D_MODEL ** -0.5),
        'b_mod': nrm((L_, N_MOD * D_MODEL), 0.02),
        'norm1_g': gain((L_, D_MODEL)),
        'norm2_g': gain((L_, D_MODEL)),
        'w_in': nrm((L_, D_MODEL, D_IN), D_MODEL ** -0.5),
        'pool_w': nrm((L_, len(POOL_WINDOWS), POOL_GROUP, POOL_GROUP), POOL_GROUP ** -0.5),
        'pool_scale': 1.0 + nrm((L_, POOL_WIDTH), 0.1),
        'pool_out': nrm((L_, POOL_WIDTH, D_MODEL), POOL_WIDTH ** -0.5),
        'hy_conv_w': nrm((L_, 3, 3 * HY_WIDTH), 3 ** -0.5),
        'hy_conv_b': nrm((L_, 3 * HY_WIDTH), 0.02),
        'hy_f_w1': nrm((L_, HY_EMB, HY_FILTER_HIDDEN), HY_EMB ** -0.5),
        'hy_f_b1': nrm((L_, HY_FILTER_HIDDEN), 0.1),
        'hy_f_freq1': 1.0 + nrm((L_, HY_FILTER_HIDDEN), 0.1),
        'hy_f_w2': nrm((L_, HY_FILTER_HIDDEN, HY_FILTER_HIDDEN), HY_FILTER_HIDDEN ** -0.5),
        'hy_f_b2': nrm((L_, HY_FILTER_HIDDEN), 0.1),
        'hy_f_freq2': 1.0 + nrm((L_, HY_FILTER_HIDDEN), 0.1),
        'hy_f_w3': nrm((L_, HY_FILTER_HIDDEN, 2 * HY_WIDTH), HY_FILTER_HIDDEN ** -0.5),
        'hy_decay': jax.random.uniform(next(ks), (L_, 2, HY_WIDTH), f32, 3.0, 15.0),
        'hy_bias': nrm((L_, HY_WIDTH), 0.5),
        'hy_out': nrm((L_, HY_WIDTH, D_MODEL), HY_WIDTH ** -0.5),
        'q_norm_g': gain((L_, Q_LORA)),
        'w_uq': nrm((L_, Q_LORA, MLA_HEADS * QK_DIM), Q_LORA ** -0.5),
        'kv_norm_g': gain((L_, KV_LORA)),
        'w_ukv': nrm((L_, KV_LORA, MLA_HEADS * (QK_NOPE + V_HEAD)), KV_LORA ** -0.5),
        'w_o': nrm((L_, MLA_HEADS * V_HEAD, D_MODEL), (MLA_HEADS * V_HEAD) ** -0.5),
        'w_out': nrm((L_, D_MODEL, D_MODEL), D_MODEL ** -0.5),
        'w_ff1': nrm((L_, D_MODEL, D_FF), D_MODEL ** -0.5),
        'w_ff2': nrm((L_, D_FF, D_MODEL), D_FF ** -0.5),
        'final_g': gain((D_MODEL,)),
    }

def reference(x, c, ctx, c_ctx, w_mod, b_mod, norm1_g, norm2_g, w_in, pool_w, pool_scale, pool_out,
              hy_conv_w, hy_conv_b, hy_f_w1, hy_f_b1, hy_f_freq1, hy_f_w2, hy_f_b2, hy_f_freq2, hy_f_w3,
              hy_decay, hy_bias, hy_out, q_norm_g, w_uq, kv_norm_g, w_ukv, w_o, w_out, w_ff1, w_ff2,
              final_g):
    ROWS = x.shape[1] // GRID_W
    cos, sin = axial_rope_tables(ROWS)
    s_lat = jax.nn.silu(c)
    s_ctx = jax.nn.silu(c_ctx)
    h, hc = x, ctx
    for l in range(DEPTH):
        lp = {
            'pool_w': pool_w[l], 'pool_scale': pool_scale[l], 'pool_out': pool_out[l],
            'hy_conv_w': hy_conv_w[l], 'hy_conv_b': hy_conv_b[l],
            'hy_f_w1': hy_f_w1[l], 'hy_f_b1': hy_f_b1[l], 'hy_f_freq1': hy_f_freq1[l],
            'hy_f_w2': hy_f_w2[l], 'hy_f_b2': hy_f_b2[l], 'hy_f_freq2': hy_f_freq2[l],
            'hy_f_w3': hy_f_w3[l], 'hy_decay': hy_decay[l], 'hy_bias': hy_bias[l], 'hy_out': hy_out[l],
            'q_norm_g': q_norm_g[l], 'w_uq': w_uq[l], 'kv_norm_g': kv_norm_g[l], 'w_ukv': w_ukv[l],
            'w_o': w_o[l], 'w_out': w_out[l],
        }
        last = l == DEPTH - 1
        sh1, sc1, g1, sh2, sc2, g2 = jnp.split((s_lat @ w_mod[l] + b_mod[l])[:, None, :], N_MOD, axis=-1)
        mod_c = s_ctx @ w_mod[l] + b_mod[l]
        sh1c, sc1c = mod_c[:D_MODEL], mod_c[D_MODEL:2 * D_MODEL]
        xn = rmsnorm(h, norm1_g[l]) * (1 + sc1) + sh1
        xnc = rmsnorm(hc, norm1_g[l]) * (1 + sc1c) + sh1c
        if last:
            proj_c = None
            ckv_c = xnc @ w_in[l][:, OFF_KV:OFF_GATE]
        else:
            proj_c = xnc @ w_in[l]
            ckv_c = proj_c[..., OFF_KV:OFF_GATE]
        k_c, v_c = mla_kv(ckv_c, kv_norm_g[l], w_ukv[l], None, None)
        h = h + g1 * token_mix(xn @ w_in[l], k_c, v_c, lp, cos, sin)
        h = h + g2 * sq_relu_mlp(rmsnorm(h, norm2_g[l]) * (1 + sc2) + sh2, w_ff1[l], w_ff2[l])
        if not last:
            g1c, sh2c, sc2c, g2c = jnp.split(mod_c[2 * D_MODEL:], 4)
            hc = hc + g1c * token_mix(proj_c, k_c, v_c, lp, None, None)
            hc = hc + g2c * sq_relu_mlp(rmsnorm(hc, norm2_g[l]) * (1 + sc2c) + sh2c, w_ff1[l], w_ff2[l])
    return rmsnorm(h, final_g)


_drawn_inputs = setup_inputs


def setup_inputs(seed=0):
    import zlib

    import numpy as np

    out = dict(_drawn_inputs(seed))
    spreads = {}
    factors = {'ctx': 4.965,
     'norm1_g': 8.0,
     'norm2_g': 35.728,
     'pool_scale': 12.507,
     'hy_conv_b': 8.0,
     'hy_f_b1': 8.0,
     'hy_f_freq1': 8.0,
     'hy_f_b2': 8.0,
     'hy_f_freq2': 8.0,
     'hy_decay': 6.828,
     'q_norm_g': 51.543,
     'w_uq': 2.795,
     'kv_norm_g': 53.289,
     'final_g': 2.729}
    for name, (base, spread) in spreads.items():
        noise = np.random.default_rng([zlib.crc32(name.encode()), seed]).standard_normal(out[name].shape)
        drawn = base * np.exp(spread * noise) if base else spread * noise
        out[name] = jnp.asarray(drawn.astype(out[name].dtype))
    for name, factor in factors.items():
        out[name] = (out[name] * factor).astype(out[name].dtype)
    return out
```

```python
import numpy as np

import concourse.bass as bass
from concourse import mybir
from contextlib import ExitStack

D = 1024
KB = D // 128
GATE_PARTS = {"c0": 0, "c1": 4, "a0": 0, "a1": 2, "a2": 4, "b0": 0, "b1": 3, "b2": 6}
B_PARTS = ("b0", "b1", "b2")
SEQ = 256
CTX = 256
T = SEQ + CTX
DEPTH = 2
EPS = 1e-6
POOL_WINDOWS = (2, 4, 8, 16)
HY = 512
HYB = HY // 128
HY_EMB = 33
HIDDEN = 64
HEADS = 8
NOPE = 64
ROPE = 32
QK = NOPE + ROPE
VH = 64
QL = 384
QB = QL // 128
KVL = 256
KVB = KVL // 128
SCALE = QK ** -0.5
GRID_W = 64
FF = 4 * D
OFF_HY = 512
OFF_Q = OFF_HY + 3 * HY
OFF_KV = OFF_Q + QL
OFF_GATE = OFF_KV + KVL + ROPE
VECTORS = 6
GROUPS = DEPTH * VECTORS
SLOTS = 4
AHEAD = 3
PAD = 8
NFREQ = 2 * SEQ // 2



def _phases():
    layers = []
    for layer in range(DEPTH):
        one = "mMmMmMmmMmMmMmMM" if layer == 0 else "M" * 8
        two = ("MmmmMmmmMmmM" * 2, 1) if layer == 0 else ("MMMM", 2)
        parts = ("MmmmMmmm", "MmmM", "MmmmMmmmMmmM") if layer == 0 else ("MM", "MM", "MMMM")
        ff = (one, 2)
        first = [(f"mod{i}", "mmmm", 1) for i in range(4)] if layer == 0 else []
        layers += [(layer, *p) for p in first + [
            ("q", "MMM", 1), ("kv", "MM", 1), ("kpe", "M", 1),
            ("gate_c0", "MMMM", 1),
            ("uq", "MMM", 1), ("ukv", "MM", 1), ("gate_c1", "MMMM", 1),
            ("wo", "MMMM", 1),
            ("pool", "MMMM", 1), ("gate_a0", parts[0], 1), ("gate_a1", parts[1], 1), ("pool_w", "M", 1),
            ("gate_a2", parts[2], 1), ("pool_out", "MMMM", 1),
            ("hy", "MMMM", 3), ("gate_b0", "MMM", 1), ("gate_b1", "MMM", 1), ("gate_b2", "MM", 1),
            ("hy_out", "MMMM", 1),
            ("w_out", *two),
            ("ff1a", *ff), ("ff2a", *ff),
            ("ff1b", *ff), ("ff2b", "M" * 8, 2),
        ]]
    return layers


BY_ACT = (*("gate_" + b for b in GATE_PARTS), "pool", "ff1a", "ff1b")
BANKS_OF = {"wo": 2, "pool_out": 2, "hy_out": 2, "ff2a": 0.5, "ff2b": 0.5, "uq": 2, "ukv": 4, "pool_w": 4}


class Phase:

    def __init__(self, layer, name, pattern, bodies, g0, act0, dve0, mod0, part0):
        self.layer, self.name, self.pattern, self.bodies = layer, name, pattern, bodies
        self.g0, self.act0, self.dve0, self.mod0, self.part0 = g0, act0, dve0, mod0, part0
        self.per_unit = max(1, BANKS_OF.get(name, 1))
        self.size = len(pattern)
        self.mains = pattern.count("M")
        self.mods = pattern.count("m")
        self.units = self.size * bodies
        self.parts = (self.per_unit - 1) * self.mains * bodies
        self.results = int(self.mains * bodies * BANKS_OF.get(name, 1))

    def places(self):
        count = {"M": 0, "m": 0}
        for j, kind in enumerate(self.pattern):
            yield j, kind, count[kind]
            count[kind] += 1


def plan():
    out, g, act, dve, mod, part = {}, 0, 0, 0, 0, 0
    for layer, name, pattern, bodies in _phases():
        p = Phase(layer, name, pattern, bodies, g, act, dve, mod, part)
        out[layer, name] = p
        g += p.units
        mod += p.mods * bodies
        part += p.parts
        if name in BY_ACT:
            act += p.results
        else:
            dve += p.results
    assert mod == KB * GROUPS
    return out, g


PHASES, UNITS = plan()

_COLS, _AT = {}, 0
for _name, _n in [("c", 2 * KB), ("gain", 4 * KB * 2), ("final_g", KB), ("pool_scale", DEPTH * 4),
                  ("conv_w", DEPTH * 3 * 3 * HYB), ("conv_b", DEPTH * 3 * HYB), ("hy_bias", DEPTH * HYB),
                  ("q_g", DEPTH * QB), ("kv_g", DEPTH * KVB), ("b_mod", GROUPS * KB * 2),
                  ("f_b", 2), ("f_freq", 2), ("neg_t", 2), ("not_first", 2), ("eps", 1)]:
    _COLS[_name] = (_AT, _n)
    _AT += _n
PARAMS = _AT
CONSTS = 3 * 128 + 2 * SEQ
FTAB = NFREQ + NFREQ + 128 + 128
FILT = 5 * HY
TWO_PI = 2 * np.pi
TWO_PI_1 = 6.28125
TWO_PI_2 = float(np.float32(np.round((TWO_PI - TWO_PI_1) * 2**21) / 2**21))
TWO_PI_3 = float(np.float32(TWO_PI - TWO_PI_1 - TWO_PI_2))
ROUNDER = 1.5 * 2**23
PI_BELOW = float(np.nextafter(np.float32(np.pi), np.float32(0)))


def backbone(nc, x_in, units_in, params_in, consts_in, fwd_in, inv_in, counts_in, emb_in, f_w12_in,
             f_w3_in, decay_in, filt_scratch, out):
    F, R = mybir.dt.float32, mybir.dt.float32r
    ALU, ACT, AX = mybir.AluOpType, mybir.ActivationFunctionType, mybir.AxisListType

    ctx = ExitStack()
    with ctx:
        def alloc(scope, name, shape, dt=F):
            return scope.enter_context(nc.sbuf_tensor(name, [128, *shape], dt))

        def sem(name):
            return ctx.enter_context(nc.semaphore(name))

        def sems(name, n=DEPTH):
            return [sem(f"{name}_{i}") for i in range(n)]

        h = alloc(ctx, "h", (KB, T))
        xh = alloc(ctx, "xh", (KB, T), R)
        xl = alloc(ctx, "xl", (KB, T), R)
        raw = alloc(ctx, "raw", (SLOTS, 1024))
        wh = alloc(ctx, "wh", (SLOTS, 1024), R)
        wl = alloc(ctx, "wl", (SLOTS, 1024), R)
        sq_sum = alloc(ctx, "sq_sum", (T,))
        sq = alloc(ctx, "sq", (2, T))
        rstd = alloc(ctx, "rstd", (T,))
        params = alloc(ctx, "params", (PARAMS,))
        consts = alloc(ctx, "consts", (CONSTS,))
        mods = alloc(ctx, "mods", (GROUPS, KB, 2))
        mod_rows = alloc(ctx, "mod_rows", (D,))
        mod_sum = alloc(ctx, "mod_sum", (KB, 2))
        scales = alloc(ctx, "scales", (4, KB, 2))
        silu = alloc(ctx, "silu", (KB, 2))
        silu_split = alloc(ctx, "silu_split", (KB, 4), R)
        small = alloc(ctx, "small", (16,))

        def param(name, *shape):
            at, n = _COLS[name]
            v = params[:, at:at + n]
            if len(shape) == 2:
                return v.rearrange("p (a b) -> p a b", b=shape[1])
            if len(shape) == 3:
                return v.rearrange("p (a b c) -> p a b c", b=shape[1], c=shape[2])
            return v

        gains = param("gain", 4, KB, 2)
        final_g = param("final_g")
        pool_scale = param("pool_scale", DEPTH, 4)
        conv_w = param("conv_w", DEPTH, 3, 3 * HYB)
        conv_b = param("conv_b", DEPTH, 3 * HYB)
        hy_bias = param("hy_bias", DEPTH, HYB)
        q_g = param("q_g", DEPTH, QB)
        kv_g = param("kv_g", DEPTH, KVB)
        b_mod = param("b_mod", GROUPS, KB, 2)
        f_b, f_freq = param("f_b"), param("f_freq")
        neg_t, not_first, eps = param("neg_t"), param("not_first"), param("eps")
        ident, ones, rot = consts[:, 0:128], consts[:, 128:256], consts[:, 256:384]
        cos, sin = consts[:, 384:384 + SEQ], consts[:, 384 + SEQ:384 + 2 * SEQ]

        KBYTE = 256
        with ExitStack() as s:
            lat_sq = alloc(s, "lat_sq", (QB + KVB, T))
            decay = alloc(s, "decay", (2 * HY,))
            alloc(s, "pad_a1", (2 * KBYTE,))
            cqh = alloc(s, "cqh", (QB, T), R)
            cql = alloc(s, "cql", (QB, T), R)
            rq = alloc(s, "rq", (T,))
            rkv = alloc(s, "rkv", (T,))
            ckh = alloc(s, "ckh", (KVB, T), R)
            ckl = alloc(s, "ckl", (KVB, T), R)
            ftab0 = alloc(s, "ftab0", (2, FTAB))
            k_pe_raw = alloc(s, "k_pe_raw", (T,))
            emb = alloc(s, "emb", (SEQ,))
            f_w12 = alloc(s, "f_w12", (2, DEPTH * HIDDEN))
            f_w3 = alloc(s, "f_w3", (2 * HY,))
            f_arg = alloc(s, "f_arg", (SEQ,))
            f_turn = alloc(s, "f_turn", (SEQ,))
            f_hid = alloc(s, "f_hid", (SEQ,))
            f_hid2 = alloc(s, "f_hid2", (SEQ,))
            f_rl1 = alloc(s, "f_rl1", (HY,))
            envelope = alloc(s, "envelope", (2, 2 * HY))
            f_even = alloc(s, "f_even", (2, HY))
            f_odd = alloc(s, "f_odd", (2, HY))
            filt0 = alloc(s, "filt0", (FILT,))
        with ExitStack() as s:
            alloc(s, "pad_n", (16 * KBYTE,))
            normed = alloc(s, "normed", (KB, T))
        with ExitStack() as s:
            alloc(s, "pad_r", (40 * KBYTE,))
            q_pe = alloc(s, "q_pe", (2, T))
            k_pe = alloc(s, "k_pe", (T,))
        with ExitStack() as s:
            sig = alloc(s, "sig", (KB, T))
            probs = alloc(s, "probs", (4, T))
            probs_t = alloc(s, "probs_t", (2, 4, SEQ))
            fh = alloc(s, "fh", (4, T), R)
            fl = alloc(s, "fl", (4, T), R)
            q_t = alloc(s, "q_t", (HEADS, T))
            k_t = alloc(s, "k_t", (HEADS, T))
            v_t = alloc(s, "v_t", (T // 128, HEADS * VH))
            roped = sq[:, :, :].rearrange("p a (b t) -> p a b t", t=SEQ)
        with ExitStack() as s:
            alloc(s, "pad_c", (16 * KBYTE,))
            y = alloc(s, "y", (KB, T))
            alloc(s, "pad_d", (16 * KBYTE,))
            padded = alloc(s, "padded", (4, 2, SEQ + 2 * PAD))
            sums = alloc(s, "sums", (2, 2, SEQ + 2 * PAD))
            uh = alloc(s, "uh", (4, T), R)
            ul = alloc(s, "ul", (4, T), R)
            counts = alloc(s, "counts", (4, 2, SEQ))
            gated = alloc(s, "gated", (2, T))
        with ExitStack() as s:
            alloc(s, "pad_e", (32 * KBYTE,))
            z_t = alloc(s, "z_t", (T // 128, HY))
            alloc(s, "pad_f", (4 * KBYTE,))
            spec_tmp = alloc(s, "spec_tmp", (2, HY))
            x0 = alloc(s, "x0", (HYB, T))
            z = alloc(s, "z", (HYB, T))
            spec = alloc(s, "spec", (4, HY))
            ftab = alloc(s, "ftab", (2, FTAB))
            itab = alloc(s, "itab", (4, SEQ))
            filt = alloc(s, "filt", (FILT,))
            conv_v = sq[:, 0, :]
            mixh, mixl = (v[:, :, :].rearrange("p a b -> p (a b)").rearrange("p (s c t) -> p s c t", s=2, t=SEQ) for v in (fh, fl))
            mix = sq[:, :, :].rearrange("p a b -> p (a b)").rearrange("p (c t) -> p c t", t=SEQ)
        with ExitStack() as s:
            hid_h = alloc(s, "hid_h", (16, T), R)
            hid_l = alloc(s, "hid_l", (16, T), R)
            relu = alloc(s, "relu", (2, T))
            relu2 = alloc(s, "relu2", (2, T))

        S_BANKS = (4, 5, 2, 3)
        neg_max, row_sum = small[:, 8:12], small[:, 12:16]
        ps = ctx.enter_context(nc.psum_tensor("ps", [128, 8, 512], F))

        params_in_s, consts_in_s, h_in_s = sem("params_loaded"), sem("consts_loaded"), sem("h_loaded")
        sine_in_s, f_w3_in_s, ftab_in_s = sem("sine_inputs_loaded"), sem("f_w3_loaded"), sem("ftab_loaded")
        decay_in_s = sems("decay_loaded")
        unit_loaded = sems("unit_loaded", SLOTS)
        hi_ready, lo_ready = sem("weight_hi_ready"), sem("weight_lo_ready")
        unit_done = sem("unit_multiplied")
        part_done = sem("part_multiplied")
        act_bank_free = sem("act_bank_free")
        dve_bank_free = sem("dve_bank_free")
        mod_copied = sem("mod_rows_copied")
        mod_turned = sem("mod_rows_turned")
        mod_added = sem("mod_added")
        mod_ready = sem("mod_ready")
        silu_sig, silu_ready, silu_hi, silu_lo = (sem(n) for n in ("silu_sig", "silu_ready", "silu_hi", "silu_lo"))
        h_squared, squares_added, sumsq_ready = sem("h_squared"), sem("squares_added"), sem("sumsq_ready")
        last_squared = sem("last_block_squared")
        std_ready, rstd_ready = sem("std_ready"), sem("rstd_ready")
        normed_dve, normed_pool = sem("normed_by_vector"), sem("normed_by_gpsimd")
        x_hi, x_split = sem("x_hi_ready"), sem("x_split")
        dve_step = sem("dve_step")
        pool_step = sem("pool_step")
        act_step = sem("act_step")
        f_pre, f_arg_ready, f_sin = sem("f_pre"), sem("f_arg_ready"), sem("f_sin")
        f_env, f_taps, f_parts, f_abs = sems("f_env"), sems("f_taps"), sems("f_parts"), sems("f_abs")
        f_spec, f_l1, f_scaled, f_saved = sems("f_spec"), sems("f_l1"), sems("f_scaled"), sems("f_saved")
        lat_sq_ready = sems("lat_sq_ready")
        lat_sumsq, lat_std, lat_rstd = sems("lat_sumsq"), sems("lat_std"), sems("lat_rstd")
        kpe_rotated, kpe_ready, kpe_spread = sems("kpe_rotated"), sems("kpe_ready"), sems("kpe_spread")
        q_ctx_ready = sem("q_ctx_ready")
        qpe_rotated, q_ready = sems("qpe_rotated"), sems("q_ready")
        scores_ready, max_ready, exp_done, probs_ready = (sems(n) for n in ("scores_ready", "max_ready", "exp_done", "probs_ready"))
        transposed, pt_act, pt_dve, pv_done, o_ready = (sems(n) for n in ("transposed", "pt_act", "pt_dve", "pv_done", "o_ready"))
        y_added = sems("y_added")
        y_hi, y_split = sems("y_hi"), sems("y_split")
        counts_loaded, pool_mean, u_hi, u_split = (sems(n) for n in ("counts_loaded", "pool_mean", "u_hi", "u_split"))
        pads_clear, pool_hi = sems("pads_clear"), sems("pool_hi")
        tables_loaded, conv_mid, zv_ready, z_transposed, z_copied = (sems(n) for n in ("tables_loaded", "conv_mid", "zv_ready", "z_transposed", "z_copied"))
        z_spec, z_cross, spec_ready, conv_done, hy_mixed, hy_hi, hy_ready = (sems(n) for n in ("z_spec", "z_cross", "spec_ready", "conv_done", "hy_mixed", "hy_hi", "hy_ready"))
        spec_tmp_ready = sems("spec_tmp_ready")
        relu2_ready, hid_hi, hid_ready = sem("relu2_ready"), sem("hid_hi"), sem("hid_ready")
        out_stored = sem("out_stored")

        def streams(layer):
            return [(0, slice(0, SEQ)), (1, slice(SEQ, T))] if layer == 0 else [(0, slice(0, SEQ))]

        def drained(layer, name, count=None):
            p = PHASES[layer, name]
            return 2 + (p.act0 if name in BY_ACT else p.dve0) + (p.results if count is None else count)

        def group_of(p, it, i):
            at = p.mod0 + i
            return it * (p.mods // KB) + at // KB, at % KB

        def mod_banks(p):
            return (0, 1) if p.name.startswith("mod") else (4, 5)

        def vector_ends(p, j):
            m = p.pattern[:j + 1].count("m") - 1
            if p.name.startswith("mod"):
                return m if (p.mod0 + m) % KB == KB - 1 else None
            return m if j and p.pattern[j - 1:j + 1] == "mM" and (p.mod0 + m) % KB == KB - 1 else None

        def wait_result(engine, p, j, i):
            if i == p.per_unit - 1:
                engine.wait_ge(unit_done, p.g0 + j + 1)
            else:
                engine.wait_ge(part_done, p.part0 + j * (p.per_unit - 1) + i + 1)

        def width(layer):
            return T if layer == 0 else SEQ

        def gate_drained(layer, b, m):
            return drained(layer, f"gate_{b}0", m + 1)

        def by_stream(v):
            return v.rearrange("p (s t) -> p s t", t=SEQ)

        def walk(engine, phase, body):
            bodies = phase.bodies
            if phase.g0 + phase.units == UNITS:
                with engine.Fori(0, bodies - 1) as it:
                    body(it)
                body(bodies - 1)
            elif bodies == 1:
                body(0)
            else:
                with engine.Fori(0, bodies) as it:
                    body(it)

        def beyond(phase, it, j):
            return isinstance(it, int) and it * phase.size + phase.g0 + j + AHEAD >= UNITS

        def unit(phase, it, j, ahead=0):
            return it * phase.size + (phase.g0 + j + ahead)

        def loaded_value(phase, it, j, ahead):
            at = phase.g0 + j + ahead
            if phase.bodies == 1:
                return 16 * (at // SLOTS + 1)
            assert phase.size % SLOTS == 0
            return it * (16 * phase.size // SLOTS) + 16 * (at // SLOTS + 1)

        NORM_T = (T, T, T, SEQ, SEQ)


        SUMSQ_BANK = (2, 6, 6, 6, 6)

        def squared_before(v):
            return (KB - 1) + (KB - 2) * (v - 1) if v else 0

        def added_before(v):
            return KB + (KB - 2) * (v - 1) if v else 0

        BY_POOL = (3, 7)

        def await_normed(engine, v, m):
            if m in BY_POOL:
                engine.wait_ge(normed_pool, len(BY_POOL) * v + BY_POOL.index(m) + 1)
            else:
                engine.wait_ge(normed_dve, (KB - len(BY_POOL)) * v + m + 1 - sum(b < m for b in BY_POOL))

        def norm_scale(v, m, s):
            return scales[:, v, m, s:s + 1] if v < 2 * DEPTH else final_g[:, m:m + 1]

        def normed_at(v, m, t):
            return (normed if v < 2 * DEPTH else h)[:, m, t]

        block = ctx.enter_context(nc.Block())

        @block.sync
        def _(sp):
            sp.dma_start(params[:, :], params_in).then_inc(params_in_s, 16)
            for s in range(SLOTS):
                sp.dma_start(raw[:, s, :], units_in[s]).then_inc(unit_loaded[s], 16)
            with sp.Fori(1, UNITS // SLOTS) as it:
                for s in range(SLOTS):
                    sp.wait_ge(lo_ready, it * SLOTS + (s + 1 - SLOTS))
                    sp.dma_start(raw[:, s, :], units_in[it * SLOTS + s]).then_inc(unit_loaded[s], 16)
            for m in BY_POOL[-1], KB - 2:
                await_normed(sp, 2 * DEPTH, m)
            sp.dma_start(out, h[:, :, 0:SEQ]).then_inc(out_stored, 16)
            sp.wait_ge(out_stored, 16)

        @block.gpsimd
        def _(pool):
            steps = [0]

            def chained(instruction):
                steps[0] += 1
                instruction.then_inc(pool_step, 1)
                pool.wait_ge(pool_step, steps[0])

            pool.dma_start(emb[0:HY_EMB, :], emb_in).then_inc(sine_in_s, 16)
            pool.dma_start(f_w12[:, :, :], f_w12_in).then_inc(sine_in_s, 16)
            pool.dma_start(consts[:, :], consts_in).then_inc(consts_in_s, 16)
            pool.dma_start(f_w3[:, :], f_w3_in).then_inc(f_w3_in_s, 16)
            pool.dma_start(decay[:, :], decay_in[0:1, :].broadcast_to([128, 2 * HY])).then_inc(decay_in_s[0], 16)
            pool.dma_start(h[:, :, :], x_in).then_inc(h_in_s, 16)

            def squares(v, layer=None, name=None):
                n = NORM_T[v]
                for m in range(KB if v == 0 else KB - 1):
                    if v:
                        pool.wait_ge(dve_bank_free, drained(layer, name, m + 1))
                    if m == 0:
                        pool.tensor_tensor(sq_sum[:, 0:n], h[:, 0, 0:n], h[:, 0, 0:n], ALU.mult).then_inc(squares_added, 1)
                        continue
                    pool.tensor_tensor(sq[:, m % 2, 0:n], h[:, m, 0:n], h[:, m, 0:n], ALU.mult).then_inc(h_squared, 1)
                    if v and m == KB - 2:
                        continue
                    pool.wait_ge(h_squared, squared_before(v) + m)
                    pool.wait_ge(squares_added, added_before(v) + m)
                    pool.tensor_tensor(sq_sum[:, 0:n], sq_sum[:, 0:n], sq[:, m % 2, 0:n], ALU.add).then_inc(squares_added, 1)

            def apply_rstd(v):
                pool.wait_ge(rstd_ready, v + 1)
                n = NORM_T[v]
                for m in BY_POOL:
                    chained(pool.tensor_tensor(normed_at(v, m, slice(0, n)), h[:, m, 0:n], rstd[:, 0:n], ALU.mult))
                    for s in range(n // SEQ):
                        dst = normed_at(v, m, slice(s * SEQ, (s + 1) * SEQ))
                        last = pool.tensor_scalar(dst, dst, norm_scale(v, m, s), None, ALU.mult)
                    last.then_inc(normed_pool, 1)

            def add_branch(layer, name):
                n = width(layer)
                for m in range(KB):
                    pool.wait_ge(dve_bank_free, drained(layer, name, m + 1))
                    pool.tensor_tensor(y[:, m, 0:n], y[:, m, 0:n], gated[:, m % 2, 0:n], ALU.add).then_inc(y_added[layer], 1)

            pool.wait_ge(h_in_s, 16)
            squares(0)
            pool.dma_start(ftab0[:, :, :], fwd_in).then_inc(ftab_in_s, 16)
            pool.wait_ge(f_env[0], 2)
            pool.dma_start(decay[:, :], decay_in[1:2, :].broadcast_to([128, 2 * HY])).then_inc(decay_in_s[1], 16)
            apply_rstd(0)
            for layer in range(DEPTH):
                n = width(layer)
                ns = n // SEQ
                if layer == 0:
                    for f in range(DEPTH):
                        pool.wait_ge(f_scaled[f], 5)
                        pool.dma_start(filt_scratch[f], filt0[:, :]).then_inc(f_saved[f], 16)
                if ns == 2:
                    pool.wait_ge(dve_bank_free, drained(layer, "uq", 2))
                    for hd in range(HEADS):
                        pool.tensor_copy(q_t[NOPE:QK, hd, SEQ:T], q_pe[32 * (hd % 4):32 * (hd % 4) + 32, hd // 4, SEQ:T])\
                            .then_inc(q_ctx_ready, 1)
                pool.wait_ge(o_ready[layer], HEADS // 2 * ns)
                pool.dma_start(counts[:, :, :, :], counts_in).then_inc(counts_loaded[layer], 16)
                pool.memset(padded[:, :, :, 0:PAD], 0.0).then_inc(pads_clear[layer], 1)
                pool.memset(padded[:, :, :, PAD + SEQ:], 0.0).then_inc(pads_clear[layer], 1)
                pool.wait_ge(counts_loaded[layer], 16)
                pool.wait_ge(pads_clear[layer], 2)
                for g, w in enumerate(POOL_WINDOWS):
                    pool.wait_ge(act_bank_free, drained(layer, "pool", g + 1))
                    if g:
                        pool.wait_ge(pool_mean[layer], g)
                    src, step, length = padded[:, g, 0:ns, :], 1, SEQ + 2 * PAD
                    for b in range(g + 1):
                        length -= step
                        dst = sums[:, b % 2, 0:ns, :]
                        chained(pool.tensor_tensor(dst[:, :, 0:length], src[:, :, 0:length],
                                                   src[:, :, step:step + length], ALU.add))
                        src, step = dst, 2 * step
                    at = PAD - w // 2
                    mean = sums[:, (g + 1) % 2, 0:ns, 0:SEQ]
                    chained(pool.tensor_tensor(mean, src[:, :, at:at + SEQ], counts[:, g, 0:ns, :], ALU.mult))
                    own = padded[:, g, 0:ns, PAD:PAD + SEQ]
                    pool.tensor_tensor(own, mean, own, ALU.subtract).then_inc(pool_mean[layer], 1)
                add_branch(layer, "pool_out")
                pool.wait_ge(dve_bank_free, drained(layer, "pool_w"))
                pool.wait_ge(y_added[layer], KB)
                pool.wait_ge(f_saved[layer], 16)
                pool.dma_start(ftab[:, :, :], fwd_in).then_inc(tables_loaded[layer], 16)
                pool.dma_start(itab[:, :, :], inv_in).then_inc(tables_loaded[layer], 16)
                pool.dma_start(filt[:, :], filt_scratch[layer]).then_inc(tables_loaded[layer], 16)
                for s in range(ns):
                    for i in range(4):
                        pool.wait_ge(z_cross[layer], 4 * s + i + 1)
                        pool.wait_ge(spec_tmp_ready[layer], 4 * s + i + 1)
                        pool.tensor_tensor(spec[:, i, :], spec[:, i, :], spec_tmp[:, i % 2, :],
                                           ALU.subtract if i < 2 else ALU.add).then_inc(spec_ready[layer], 1)
                add_branch(layer, "hy_out")
                squares(2 * layer + 1, layer, "w_out")
                apply_rstd(2 * layer + 1)
                squares(2 * layer + 2, layer, "ff2b")
                apply_rstd(2 * layer + 2)

        @block.scalar
        def _(act):
            steps = [0]

            def chained(instruction):
                steps[0] += 1
                instruction.then_inc(act_step, 1)
                act.wait_ge(act_step, steps[0])

            def split(slot, loaded):
                act.wait_ge(unit_loaded[slot], loaded)
                act.activation(wh[:, slot, :], raw[:, slot, :], ACT.Copy).then_inc(hi_ready, 1)

            def ahead(p, it, j):
                if not beyond(p, it, j):
                    if p.g0 + j or not isinstance(it, int):
                        act.wait_ge(unit_done, unit(p, it, j))
                    split((p.g0 + j + AHEAD) % SLOTS, loaded_value(p, it, j, AHEAD))

            def hi_copy(dst, src, wait, value, signal):
                act.wait_ge(wait, value)
                act.activation(dst, src, ACT.Copy).then_inc(signal, 1)

            def std(v):
                n = NORM_T[v]
                if v:
                    act.wait_ge(dve_bank_free, drained((v - 1) // 2, "w_out" if v % 2 else "ff2b"))
                    act.wait_ge(squares_added, added_before(v + 1))
                    act.activation(sq[:, 1, 0:n], h[:, KB - 1, 0:n], ACT.Square).then_inc(last_squared, 1)
                act.wait_ge(sumsq_ready, v + 1)
                act.activation(rstd[:, 0:n], ps[:, SUMSQ_BANK[v], 0:n], ACT.Sqrt, bias=eps[:, 0:1], scale=1.0 / D).then_inc(std_ready, 1)

            def norm_hi(v, m):
                shift = VECTORS * (v // 2) + 3 * (v % 2)
                await_normed(act, v, m)
                for s in range(NORM_T[v] // SEQ):
                    t = slice(s * SEQ, (s + 1) * SEQ)
                    last = act.activation(xh[:, m, t], normed[:, m, t], ACT.Identity, bias=mods[:, shift, m, s:s + 1])
                last.then_inc(x_hi, 1)

            def norm(v):
                std(v)
                for m in range(KB):
                    norm_hi(v, m)

            def copy_mod(p, it, j, i):
                if (p.mod0 + i) % KB == KB - 1:
                    act.wait_ge(unit_done, unit(p, it, j, 1))
                    for half, bank in enumerate(mod_banks(p)):
                        act.activation(mod_rows[0:4, half * 512:(half + 1) * 512], ps[0:4, bank, :], ACT.Copy).then_inc(mod_copied, 1)

            def gates(layer, b):
                p = PHASES[layer, "gate_" + b]
                n = width(layer)
                m0 = GATE_PARTS[b]

                def body(it):
                    for j, kind, i in p.places():
                        ahead(p, it, j)
                        if kind == "M":
                            act.wait_ge(unit_done, unit(p, it, j, 1))
                            act.activation(sig[:, it * p.mains + (m0 + i), 0:n], ps[:, (p.act0 + i) % 2, 0:n], ACT.Sigmoid)\
                               .then_inc(act_bank_free, 1)
                        else:
                            copy_mod(p, it, j, i)
                walk(act, p, body)

            def idle_phase(layer, name):
                p = PHASES[layer, name]

                def body(it):
                    for j, kind, i in p.places():
                        ahead(p, it, j)
                        if kind == "m":
                            copy_mod(p, it, j, i)
                walk(act, p, body)

            def straight(layer, name):
                p = PHASES[layer, name]
                for j in range(p.units):
                    if p.g0 + j >= 1:
                        act.wait_ge(unit_done, p.g0 + j)
                    at = p.g0 + j + AHEAD
                    split(at % SLOTS, 16 * (at // SLOTS + 1))
                    yield j, p

            act.wait_ge(params_in_s, 16)
            act.activation(silu[:, :, :], param("c", KB, 2), ACT.Sigmoid).then_inc(silu_sig, 1)
            hi_copy(silu_split[:, :, 0:2], silu[:, :, :], silu_ready, 1, silu_hi)
            act.activation(small[:, 0:1], params[:, 0:1], ACT.Copy).then_inc(act_bank_free, 2)
            for s in range(AHEAD):
                split(s, 16)

            def filter_sines(stage):
                act.wait_ge(f_arg_ready, stage + 1)
                act.activation((f_hid, f_hid2)[stage][:, :], f_arg[:, :], ACT.Sin).then_inc(f_sin, 1)

            def filter_envelope(f):
                act.wait_ge(decay_in_s[f], 16)
                if f:
                    act.wait_ge(f_l1[f - 1], 1)
                chained(act.activation(decay[:, :], decay[:, :], ACT.Abs))
                for tb in range(2):
                    act.activation(envelope[:, tb, :], decay[:, :], ACT.Exp, scale=neg_t[:, tb:tb + 1]).then_inc(f_env[f], 1)

            def filter_absolutes(f):
                for tb in range(2):
                    act.wait_ge(f_parts[f], 2 * tb + 2)
                    act.activation(envelope[:, tb, :], envelope[:, tb, :], ACT.Abs).then_inc(f_abs[f], 1)

            filter_sines(0)
            filter_sines(1)
            filter_envelope(0)
            for i in range(4):
                idle_phase(0, f"mod{i}")
            filter_absolutes(0)
            std(0)
            for m in range(KB):
                norm_hi(0, m)
            filter_envelope(1)

            for layer in range(DEPTH):
                n = width(layer)
                ns = n // SEQ
                i = 0
                for name, nt in (("q", n), ("kv", T)):
                    if (layer, name) == (0, "kv"):
                        filter_absolutes(1)
                    for j, p in straight(layer, name):
                        act.wait_ge(unit_done, p.g0 + j + 1)
                        act.activation(lat_sq[:, i, 0:nt], ps[:, 2 + (p.dve0 + j) % 2, 0:nt], ACT.Square).then_inc(lat_sq_ready[layer], 1)
                        i += 1
                for _ in straight(layer, "kpe"):
                    pass
                act.wait_ge(lat_sumsq[layer], 1)
                act.activation(rq[:, 0:n], ps[:, 5, 0:n], ACT.Sqrt, bias=eps[:, 0:1], scale=1.0 / QL).then_inc(lat_std[layer], 1)
                act.wait_ge(lat_sumsq[layer], 2)
                act.activation(rkv[:, :], ps[:, 6, :], ACT.Sqrt, bias=eps[:, 0:1], scale=1.0 / KVL).then_inc(lat_std[layer], 1)
                act.wait_ge(lat_sumsq[layer], 3)
                act.activation(small[:, 4:8], ps[:, 7, 0:4], ACT.Sqrt, bias=eps[:, 0:1], scale=1.0 / KVL).then_inc(lat_std[layer], 1)
                gates(layer, "c0")
                for name in ("uq", "ukv"):
                    for _ in straight(layer, name):
                        pass
                act.wait_ge(kpe_ready[layer], 1)
                for hd in range(HEADS):
                    act.activation(k_t[NOPE:QK, hd, :], k_pe[0:ROPE, :], ACT.Copy).then_inc(kpe_spread[layer], 1)
                gates(layer, "c1")
                jobs = [(hd, s) for s in range(ns) for hd in range(HEADS)]

                def exponentials(jb):
                    keys = T if jobs[jb][1] == 0 else CTX
                    if jb >= 2:
                        act.wait_ge(transposed[layer], jb - 1)
                    for qb in range(2):
                        act.wait_ge(max_ready[layer], 2 * jb + qb + 1)
                        c = 2 * (jb % 2) + qb
                        act.activation(probs[:, c, 0:keys], ps[:, S_BANKS[c], 0:keys], ACT.Exp, bias=neg_max[:, c:c + 1],
                                       accum_out=row_sum[:, c:c + 1]).then_inc(exp_done[layer], 1)

                exponentials(0)
                for jb, (hd, s) in enumerate(jobs):
                    if jb + 1 < len(jobs):
                        exponentials(jb + 1)
                    act.wait_ge(transposed[layer], jb + 1)
                    if jb >= 2:
                        act.wait_ge(pv_done[layer], jb - 1)
                    act.activation(probs_t[:, jb % 2, 0:2, :], ps[:, 6, :].rearrange("p (k q) -> p k q", q=SEQ),
                                   ACT.Copy).then_inc(pt_act[layer], 1)
                for _ in straight(layer, "wo"):
                    pass
                for j, p in straight(layer, "pool"):
                    act.wait_ge(unit_done, p.g0 + j + 1)
                    act.wait_ge(pads_clear[layer], 2)
                    act.activation(padded[:, j, 0:ns, PAD:PAD + SEQ],
                                   ps[:, (p.act0 + j) % 2, 0:n].rearrange("p (s t) -> p s t", t=SEQ),
                                   ACT.Copy).then_inc(act_bank_free, 1)
                gates(layer, "a0")
                for g in range(4):
                    hi_copy(by_stream(uh[:, g, 0:n]), padded[:, g, 0:ns, PAD:PAD + SEQ], pool_mean[layer], g + 1, u_hi[layer])
                gates(layer, "a1")
                for j, p in straight(layer, "pool_w"):
                    for g in range(4):
                        wait_result(act, p, j, g)
                        act.activation(fh[:, g, 0:n], ps[:, 2 + (p.dve0 + g) % 2, 0:n], ACT.Copy, scale=pool_scale[:, layer, g:g + 1])\
                           .then_inc(pool_hi[layer], 1)
                gates(layer, "a2")
                for _ in straight(layer, "pool_out"):
                    pass
                for third in range(3):
                    p = PHASES[layer, "hy"]
                    for i in range(HYB):
                        j = third * HYB + i
                        act.wait_ge(unit_done, p.g0 + j)
                        at = p.g0 + j + AHEAD
                        split(at % SLOTS, 16 * (at // SLOTS + 1))
                        act.wait_ge(unit_done, p.g0 + j + 1)
                        if third == 1 and i:
                            act.wait_ge(zv_ready[layer], i)
                        if third == 0 and i == 0:
                            act.wait_ge(dve_bank_free, drained(layer, "pool_w"))
                        dst = (z[:, i, 0:n], conv_v[:, 0:n], x0[:, i, 0:n])[third]
                        act.activation(dst, ps[:, 2 + (p.dve0 + j) % 2, 0:n], ACT.Identity, bias=conv_b[:, layer, j:j + 1],
                                       scale=conv_w[:, layer, 1, j:j + 1]).then_inc(conv_mid[layer], 1)
                for tb in range(2 * ns):
                    act.wait_ge(z_transposed[layer], tb + 1)
                    act.activation(z_t[:, tb, :], ps[:, 6 + tb % 2, :], ACT.Copy).then_inc(z_copied[layer], 1)
                for s, b in enumerate(B_PARTS):
                    gates(layer, b)
                    if s < ns:
                        for c in range(HYB):
                            hi_copy(mixh[:, s, c, :], mix[:, c, :], hy_mixed[layer], HYB * s + c + 1, hy_hi[layer])
                def y_hi_copy(m):
                    hi_copy(xh[:, m, 0:n], y[:, m, 0:n], y_added[layer], KB + m + 1, y_hi[layer])

                for j, p in straight(layer, "hy_out"):
                    if j:
                        y_hi_copy(2 * j - 2)
                        y_hi_copy(2 * j - 1)
                y_hi_copy(KB - 2)
                y_hi_copy(KB - 1)
                idle_phase(layer, "w_out")
                norm(2 * layer + 1)
                for half in "ab":
                    p = PHASES[layer, "ff1" + half]
                    r0 = 16 * (2 * layer + (half == "b"))

                    def hidden_hi(p, it, i, r0=r0, n=n):
                        act.wait_ge(relu2_ready, it * p.mains + (r0 + i + 3))
                        act.activation(hid_h[:, it * p.mains + i, 0:n], relu2[:, i % 2, 0:n], ACT.Copy).then_inc(hid_hi, 1)

                    def body(it, p=p, r0=r0, n=n):
                        for j, kind, i in p.places():
                            ahead(p, it, j)
                            if kind == "m":
                                copy_mod(p, it, j, i)
                                continue
                            r = it * p.mains + (r0 + i)
                            act.wait_ge(unit_done, unit(p, it, j, 1))
                            act.wait_ge(relu2_ready, r + 1)
                            act.activation(relu[:, i % 2, 0:n], ps[:, (p.act0 + i) % 2, 0:n], ACT.Relu).then_inc(act_bank_free, 1)
                            if i:
                                hidden_hi(p, it, i - 1)
                        hidden_hi(p, it, p.mains - 1)
                    walk(act, p, body)
                    idle_phase(layer, "ff2" + half)
                (norm if layer == 0 else std)(2 * layer + 2)


        @block.vector
        def _(dve):
            steps = [0]

            def chained(instruction):
                steps[0] += 1
                instruction.then_inc(dve_step, 1)
                dve.wait_ge(dve_step, steps[0])

            def split_at(g, slot):
                dve.wait_ge(hi_ready, g + 1)
                dve.tensor_tensor(wl[:, slot, :], raw[:, slot, :], wh[:, slot, :].bitcast(F), ALU.subtract).then_inc(lo_ready, 1)

            def ahead(p, it, j):
                if not beyond(p, it, j):
                    split_at(unit(p, it, j, AHEAD), (p.g0 + j + AHEAD) % SLOTS)

            def drain_mod(p, it, j):
                i = vector_ends(p, j)
                if i is None:
                    return
                v = group_of(p, it, i)[0]
                dve.wait_ge(mod_turned, v + 1)
                turned = ps[:, mod_banks(p)[0], 0:4 * KB].rearrange("p (m r) -> p m r", r=4)
                dve.tensor_tensor(mod_sum[:, :, :], turned[:, :, 0:2], b_mod[:, v, :, :], ALU.add).then_inc(mod_added, 1)
                dve.wait_ge(mod_added, v + 1)
                dve.tensor_tensor(mods[:, v, :, :], turned[:, :, 2:4], mod_sum[:, :, :], ALU.add).then_inc(mod_ready, 1)

            def loop(layer, name, drain=None):
                p = PHASES[layer, name]

                def body(it):
                    for j, kind, i in p.places():
                        ahead(p, it, j)
                        if kind == "M" and drain is not None:
                            drain(p, it, j, i)
                        drain_mod(p, it, j)
                walk(dve, p, body)

            def straight(layer, name):
                p = PHASES[layer, name]
                first_bank = 0 if name in BY_ACT else 2
                r0 = p.act0 if name in BY_ACT else p.dve0
                for j in range(p.units):
                    split_at(p.g0 + j + AHEAD, (p.g0 + j + AHEAD) % SLOTS)
                    for i in range(p.per_unit):
                        wait_result(dve, p, j, i)
                        yield j, i, p, first_bank + (r0 + j * p.per_unit + i) % 2

            def norm(v, between=None):
                n = NORM_T[v]
                streams_of = range(n // SEQ)
                shift = VECTORS * (v // 2) + 3 * (v % 2)
                split = v < 2 * DEPTH
                if split:
                    dve.wait_ge(mod_ready, shift + 2)
                    chained(dve.scalar_tensor_tensor(scales[:, v, :, :], mods[:, shift + 1, :, :], 1.0,
                                                     gains[:, v, :, :], ALU.add, ALU.mult))
                dve.wait_ge(std_ready, v + 1)
                dve.reciprocal(rstd[:, 0:n], rstd[:, 0:n]).then_inc(rstd_ready, 1)
                dve.wait_ge(rstd_ready, v + 1)

                def scale(m):
                    if m not in BY_POOL:
                        for s in streams_of:
                            t = slice(s * SEQ, (s + 1) * SEQ)
                            last = dve.scalar_tensor_tensor(normed_at(v, m, t), h[:, m, t], norm_scale(v, m, s), rstd[:, t],
                                                            ALU.mult, ALU.mult)
                        last.then_inc(normed_dve, 1)

                def lo(m):
                    dve.wait_ge(x_hi, KB * v + m + 1)
                    for s in streams_of:
                        t = slice(s * SEQ, (s + 1) * SEQ)
                        last = dve.scalar_tensor_tensor(xl[:, m, t], normed[:, m, t], mods[:, shift, m, s:s + 1],
                                                        xh[:, m, t].bitcast(F), ALU.add, ALU.subtract)
                    last.then_inc(x_split, 1)

                lead = 2
                for m in range(KB + lead):
                    if m < KB:
                        scale(m)
                    if split and m >= lead:
                        lo(m - lead)
                    if between is not None:
                        between(m)

            def hi_lo(dst_h, dst_l, src, scale):
                chained(dve.tensor_scalar(dst_h, src, scale, None, ALU.mult))
                dve.scalar_tensor_tensor(dst_l, src, scale, dst_h.bitcast(F), ALU.mult, ALU.subtract).then_inc(dve_bank_free, 1)

            def filter_sine_argument(stage):
                a, k = f_arg[:, :], f_turn[:, :]
                dve.wait_ge(f_pre, stage + 1)
                if stage:
                    dve.wait_ge(f_sin, stage)
                chained(dve.tensor_scalar(a, ps[:, 6, 0:SEQ], f_b[:, stage:stage + 1], f_freq[:, stage:stage + 1],
                                          ALU.add, ALU.mult))
                chained(dve.tensor_scalar(k, a, 1.0 / TWO_PI, ROUNDER, ALU.mult, ALU.add))
                chained(dve.tensor_scalar(k, k, ROUNDER, None, ALU.subtract))
                for part in (TWO_PI_1, TWO_PI_2, TWO_PI_3):
                    chained(dve.scalar_tensor_tensor(a, k, -part, a, ALU.mult, ALU.add))
                dve.tensor_scalar(a, a, PI_BELOW, -PI_BELOW, ALU.min, ALU.max).then_inc(f_arg_ready, 1)

            def filter_taps(f):
                dve.wait_ge(f_env[f], 2)
                for tb in range(2):
                    dve.wait_ge(f_taps[f], tb + 1)
                    fwd = ps[:, 4 + 2 * tb, :]
                    bwd = ps[:, 5 + 2 * tb, :]
                    e = envelope[:, tb, :]
                    chained(dve.tensor_tensor(e[:, 0:HY], fwd, e[:, 0:HY], ALU.mult))
                    chained(dve.scalar_tensor_tensor(e[:, HY:], bwd, not_first[:, tb:tb + 1], e[:, HY:], ALU.mult, ALU.mult))
                    dve.tensor_tensor(f_even[:, tb, :], e[:, 0:HY], e[:, HY:], ALU.add).then_inc(f_parts[f], 1)
                    dve.tensor_tensor(f_odd[:, tb, :], e[:, 0:HY], e[:, HY:], ALU.subtract).then_inc(f_parts[f], 1)

            def filter_l1(f):
                dve.wait_ge(f_l1[f], 1)
                chained(dve.reciprocal(f_rl1[:, :], ps[:, 7, :]))
                if f:
                    dve.wait_ge(f_saved[f - 1], 16)

            def filter_scaled(f, i):
                dve.wait_ge(f_spec[f], i + 1)
                dve.tensor_tensor(filt0[:, i * HY:(i + 1) * HY], ps[:, (2, 3, 4, 5, 6)[i], :], f_rl1[:, :], ALU.mult)\
                   .then_inc(f_scaled[f], 1)

            dve.memset(small[:, 1:2], 0.0).then_inc(dve_bank_free, 2)
            dve.wait_ge(silu_sig, 1)
            dve.tensor_tensor(silu[:, :, :], silu[:, :, :], param("c", KB, 2), ALU.mult).then_inc(silu_ready, 1)
            dve.wait_ge(silu_hi, 1)
            dve.tensor_tensor(silu_split[:, :, 2:4], silu[:, :, :], silu_split[:, :, 0:2].bitcast(F), ALU.subtract).then_inc(silu_lo, 1)
            for s in range(AHEAD):
                split_at(s, s)
            filter_sine_argument(0)
            filter_sine_argument(1)
            for i in range(3):
                loop(0, f"mod{i}")
            filter_taps(0)
            loop(0, "mod3")

            def filter_between(m):
                if m == 3:
                    filter_l1(0)
                elif 4 <= m < 9:
                    filter_scaled(0, m - 4)
            norm(0, filter_between)
            for layer in range(DEPTH):
                n = width(layer)
                ns = n // SEQ
                i = 0
                for name, dh, dl, g, nt in (("q", cqh, cql, q_g, n), ("kv", ckh, ckl, kv_g, T)):
                    if (layer, name) == (0, "kv"):
                        filter_taps(1)
                    for j, _, _, bank in straight(layer, name):
                        dve.wait_ge(lat_sq_ready[layer], i + 1)
                        hi_lo(dh[:, j, 0:nt], dl[:, j, 0:nt], ps[:, bank, 0:nt], g[:, layer, j:j + 1])
                        i += 1
                if layer == 0:
                    filter_l1(1)
                    for k in range(5):
                        filter_scaled(1, k)
                for _, _, _, bank in straight(layer, "kpe"):
                    dve.tensor_copy(k_pe_raw[0:ROPE, :], ps[0:ROPE, bank, :]).then_inc(dve_bank_free, 1)
                dve.wait_ge(lat_std[layer], 1)
                chained(dve.reciprocal(rq[:, 0:n], rq[:, 0:n]))
                chained(dve.tensor_scalar(rq[:, 0:n], rq[:, 0:n], SCALE, None, ALU.mult))
                dve.wait_ge(lat_std[layer], 3)
                dve.reciprocal(rkv[:, :], rkv[:, :]).then_inc(lat_rstd[layer], 1)
                dve.reciprocal(small[:, 4:8], small[:, 4:8]).then_inc(lat_rstd[layer], 1)
                loop(layer, "gate_c0")
                if layer == 0:
                    dve.wait_ge(f_saved[DEPTH - 1], 16)
                dve.wait_ge(kpe_rotated[layer], 1)
                dve.tensor_copy(k_pe[0:ROPE, SEQ:T], k_pe_raw[0:ROPE, SEQ:T])
                dve.tensor_tensor(roped[0:ROPE, 0, 0, :], k_pe_raw[0:ROPE, 0:SEQ], cos[0:ROPE, :], ALU.mult)
                chained(dve.tensor_tensor(roped[0:ROPE, 1, 0, :], ps[0:ROPE, 6, 0:SEQ], sin[0:ROPE, :], ALU.mult))
                dve.tensor_tensor(k_pe[0:ROPE, 0:SEQ], roped[0:ROPE, 0, 0, :], roped[0:ROPE, 1, 0, :], ALU.add)\
                   .then_inc(kpe_ready[layer], 1)
                dve.wait_ge(lat_rstd[layer], 2)
                for j, i, _, bank in straight(layer, "uq"):
                    b = 2 * j + i
                    if b >= 2:
                        for half in range(2):
                            rows = slice(64 * half, 64 * half + 64)
                            last = dve.tensor_tensor(q_t[0:NOPE, 2 * (b - 2) + half, 0:n], ps[rows, bank, 0:n], rq[rows, 0:n], ALU.mult)
                        last.then_inc(dve_bank_free, 1)
                    else:
                        dve.tensor_tensor(q_pe[:, b, 0:n], ps[:, bank, 0:n], rq[:, 0:n], ALU.mult).then_inc(dve_bank_free, 1)
                for j, i, _, bank in straight(layer, "ukv"):
                    if j == 0:
                        for half in range(2):
                            rows = slice(64 * half, 64 * half + 64)
                            last = dve.tensor_tensor(k_t[0:NOPE, 2 * i + half, :], ps[rows, bank, :], rkv[rows, :], ALU.mult)
                    else:
                        last = dve.tensor_scalar(v_t[:, i, :], ps[:, bank, :], small[:, 4 + i:5 + i], None, ALU.mult)
                    last.then_inc(dve_bank_free, 1)
                dve.wait_ge(qpe_rotated[layer], 1)
                dve.wait_ge(dve_bank_free, drained(layer, "uq"))
                for b in range(2):
                    dve.tensor_tensor(roped[:, 0, b, :], q_pe[:, b, 0:SEQ], cos[:, :], ALU.mult)
                    chained(dve.tensor_tensor(roped[:, 1, b, :], ps[:, 6, b * SEQ:(b + 1) * SEQ], sin[:, :], ALU.mult))
                    for i in range(4):
                        rows = slice(32 * i, 32 * i + 32)
                        done = dve.tensor_tensor(q_t[NOPE:QK, 4 * b + i, 0:SEQ], roped[rows, 0, b, :], roped[rows, 1, b, :], ALU.add)
                        if (b, i) == (1, 3):
                            done.then_inc(q_ready[layer], 1)
                        else:
                            chained(done)
                loop(layer, "gate_c1")

                jobs = [(hd, s) for s in range(ns) for hd in range(HEADS)]

                def maxima(jb):
                    keys = T if jobs[jb][1] == 0 else CTX
                    for qb in range(2):
                        dve.wait_ge(scores_ready[layer], 2 * jb + qb + 1)
                        c = 2 * (jb % 2) + qb
                        dve.tensor_reduce(neg_max[:, c:c + 1], ps[:, S_BANKS[c], 0:keys], AX.X, ALU.max, negate=True)\
                           .then_inc(max_ready[layer], 1)

                def normalise(jb):
                    keys = T if jobs[jb][1] == 0 else CTX
                    both = row_sum[:, 2 * (jb % 2):2 * (jb % 2) + 2]
                    dve.wait_ge(exp_done[layer], 2 * jb + 2)
                    chained(dve.reciprocal(both, both))
                    for qb in range(2):
                        c = 2 * (jb % 2) + qb
                        dve.tensor_scalar(probs[:, c, 0:keys], probs[:, c, 0:keys], row_sum[:, c:c + 1], None, ALU.mult)\
                           .then_inc(probs_ready[layer], 1)

                def outputs(jb):
                    hd, s = jobs[jb]
                    if hd % 2:
                        dve.wait_ge(pv_done[layer], jb + 1)
                        pair = jb // 2
                        src = ps[:, pair % 2, 0:SEQ]
                        t = slice(s * SEQ, (s + 1) * SEQ)
                        chained(dve.tensor_copy(fh[:, hd // 2, t], src))
                        dve.tensor_tensor(fl[:, hd // 2, t], src, fh[:, hd // 2, t].bitcast(F), ALU.subtract)\
                           .then_inc(o_ready[layer], 1)

                maxima(0)
                maxima(1)
                normalise(0)
                for jb in range(len(jobs)):
                    if jobs[jb][1] == 0:
                        dve.wait_ge(transposed[layer], jb + 1)
                        if jb >= 2:
                            dve.wait_ge(pv_done[layer], jb - 1)
                        dve.tensor_copy(probs_t[:, jb % 2, 2:4, :], ps[:, 7, :].rearrange("p (k q) -> p k q", q=SEQ))\
                           .then_inc(pt_dve[layer], 1)
                    if jb + 1 < len(jobs):
                        normalise(jb + 1)
                    if jb + 2 < len(jobs):
                        maxima(jb + 2)
                    if jb:
                        outputs(jb - 1)
                outputs(len(jobs) - 1)

                def branch_out(name, b):
                    first = {"c": 0, "a": 0, "b": KB}[b]
                    for j, i, p, bank in straight(layer, name):
                        m = 2 * j + i
                        dve.wait_ge(act_bank_free, gate_drained(layer, b, m))
                        if b != "c" and first + m >= 2:
                            dve.wait_ge(y_added[layer], first + m - 1)
                        dst = y[:, m, 0:n] if b == "c" else gated[:, m % 2, 0:n]
                        dve.tensor_tensor(dst, ps[:, bank, 0:n], sig[:, m, 0:n], ALU.mult).then_inc(dve_bank_free, 1)
                        if b == "b" and m >= 2:
                            y_lo(m - 2)
                    if b == "b":
                        y_lo(KB - 2)
                        y_lo(KB - 1)

                def y_lo(m):
                    dve.wait_ge(y_hi[layer], m + 1)
                    dve.tensor_tensor(xl[:, m, 0:n], y[:, m, 0:n], xh[:, m, 0:n].bitcast(F), ALU.subtract).then_inc(y_split[layer], 1)

                branch_out("wo", "c")
                for _ in straight(layer, "pool"):
                    pass
                loop(layer, "gate_a0")
                for g in range(4):
                    dve.wait_ge(u_hi[layer], g + 1)
                    dve.tensor_tensor(by_stream(ul[:, g, 0:n]), padded[:, g, 0:ns, PAD:PAD + SEQ],
                                      by_stream(uh[:, g, 0:n].bitcast(F)), ALU.subtract).then_inc(u_split[layer], 1)
                loop(layer, "gate_a1")
                for _, g, _, bank in straight(layer, "pool_w"):
                    dve.wait_ge(pool_hi[layer], g + 1)
                    dve.scalar_tensor_tensor(fl[:, g, 0:n], ps[:, bank, 0:n], pool_scale[:, layer, g:g + 1],
                                             fh[:, g, 0:n].bitcast(F), ALU.mult, ALU.subtract).then_inc(dve_bank_free, 1)
                loop(layer, "gate_a2")
                branch_out("pool_out", "a")

                def hy_unit(third, i):
                    p = PHASES[layer, "hy"]
                    j = third * HYB + i
                    split_at(p.g0 + j + AHEAD, (p.g0 + j + AHEAD) % SLOTS)
                    dve.wait_ge(conv_mid[layer], j + 1)
                    dst = (z[:, i, 0:n], conv_v[:, 0:n], x0[:, i, 0:n])[third].rearrange("p (s t) -> p s t", t=SEQ)
                    src = ps[:, 2 + (p.dve0 + j) % 2, 0:n].rearrange("p (s t) -> p s t", t=SEQ)
                    chained(dve.scalar_tensor_tensor(dst[:, :, 1:SEQ], src[:, :, 0:SEQ - 1], conv_w[:, layer, 0, j:j + 1],
                                                     dst[:, :, 1:SEQ], ALU.mult, ALU.add))
                    dve.scalar_tensor_tensor(dst[:, :, 0:SEQ - 1], src[:, :, 1:SEQ], conv_w[:, layer, 2, j:j + 1],
                                             dst[:, :, 0:SEQ - 1], ALU.mult, ALU.add).then_inc(dve_bank_free, 1)
                    if third == 1:
                        dve.wait_ge(dve_bank_free, drained(layer, "hy", j + 1))
                        dve.tensor_tensor(z[:, i, 0:n], z[:, i, 0:n], conv_v[:, 0:n], ALU.mult).then_inc(zv_ready[layer], 1)

                for third in range(3):
                    for i in range(HYB):
                        hy_unit(third, i)
                dve.wait_ge(tables_loaded[layer], 48)
                re, im = (filt[:, 0:HY], filt[:, HY:2 * HY]), (filt[:, 2 * HY:3 * HY], filt[:, 3 * HY:4 * HY])
                re_nyquist = (filt[:, 4 * HY:5 * HY], re[1])

                def spectra_product(s):
                    dve.wait_ge(z_spec[layer], 4 * (s + 1))
                    if s:
                        dve.wait_ge(conv_done[layer], HYB * s)
                    for i in range(4):
                        b = i % 2
                        zr, zi = ps[:, 4 + b, :], ps[:, 6 + b, :]
                        dve.tensor_tensor(spec[:, i, :], zr, re[b] if i < 2 else im[b], ALU.mult).then_inc(z_cross[layer], 1)
                        if 4 * s + i >= 2:
                            dve.wait_ge(spec_ready[layer], 4 * s + i - 1)
                        dve.tensor_tensor(spec_tmp[:, i % 2, :], zi, im[b] if i < 2 else re_nyquist[b], ALU.mult)\
                           .then_inc(spec_tmp_ready[layer], 1)

                def mixed(s):
                    t = slice(s * SEQ, (s + 1) * SEQ)

                    def lo(c):
                        dve.wait_ge(hy_hi[layer], HYB * s + c + 1)
                        dve.tensor_tensor(mixl[:, s, c, :], mix[:, c, :], mixh[:, s, c, :].bitcast(F), ALU.subtract).then_inc(hy_ready[layer], 1)

                    if s:
                        dve.wait_ge(hy_ready[layer], HYB * s)
                    for c in range(HYB):
                        dve.wait_ge(conv_done[layer], HYB * s + c // 2 * 2 + 2)
                        chained(dve.scalar_tensor_tensor(mix[:, c, :], z[:, c, t], hy_bias[:, layer, c:c + 1],
                                                         ps[:, 2 + c // 2, c % 2 * SEQ:(c % 2 + 1) * SEQ], ALU.mult, ALU.add))
                        dve.tensor_tensor(mix[:, c, :], mix[:, c, :], x0[:, c, t], ALU.mult).then_inc(hy_mixed[layer], 1)
                        if c:
                            lo(c - 1)
                    lo(HYB - 1)

                for s, b in enumerate(B_PARTS):
                    if s < ns:
                        spectra_product(s)
                    loop(layer, "gate_" + b)
                    if s < ns:
                        mixed(s)
                branch_out("hy_out", "b")

                def residual(gate):
                    def drain(p, it, j, i):
                        m = it * results_in(p) + i
                        bank = 2 + (p.dve0 + i) % 2
                        dve.wait_ge(unit_done, unit(p, it, j, 1))
                        for s in range(ns):
                            t = slice(s * SEQ, (s + 1) * SEQ)
                            last = dve.scalar_tensor_tensor(h[:, m, t], ps[:, bank, t], mods[:, gate, m, s:s + 1],
                                                            h[:, m, t], ALU.mult, ALU.add)
                        last.then_inc(dve_bank_free, 1)
                    return drain

                def results_in(p):
                    return p.mains if p.name == "w_out" else p.mains // 2

                def second_unit_only(drain):
                    def both(p, it, j, i):
                        if i % 2:
                            drain(p, it, j, i // 2)
                    return both

                dve.wait_ge(mod_ready, VECTORS * layer + 3)
                loop(layer, "w_out", residual(VECTORS * layer + 2))
                norm(2 * layer + 1)
                for half in "ab":
                    r0 = 16 * (2 * layer + (half == "b"))

                    def square(p, it, j, i, r0=r0):
                        r = it * p.mains + (r0 + i)
                        dve.wait_ge(hid_ready, r + 1)
                        dve.wait_ge(act_bank_free, it * p.mains + (2 + p.act0 + i + 1))
                        dve.tensor_tensor(relu2[:, i % 2, 0:n], relu[:, i % 2, 0:n], relu[:, i % 2, 0:n], ALU.mult)\
                           .then_inc(relu2_ready, 1)
                        if i:
                            hidden_lo(p, it, i - 1)
                        if i == p.mains - 1:
                            hidden_lo(p, it, i)

                    def hidden_lo(p, it, i, r0=r0):
                        dve.wait_ge(hid_hi, it * p.mains + (r0 + i + 1))
                        dve.tensor_tensor(hid_l[:, it * p.mains + i, 0:n], relu2[:, i % 2, 0:n],
                                          hid_h[:, it * p.mains + i, 0:n].bitcast(F), ALU.subtract).then_inc(hid_ready, 1)

                    if layer == 0 and half == "a":
                        dve.memset(small[:, 2:3], 0.0).then_inc(hid_ready, 2)
                        dve.memset(small[:, 3:4], 0.0).then_inc(relu2_ready, 2)
                    loop(layer, "ff1" + half, square)
                    dve.wait_ge(mod_ready, VECTORS * layer + 6)
                    loop(layer, "ff2" + half, second_unit_only(residual(VECTORS * layer + 5)))
                norm(2 * layer + 2)

        @block.tensor
        def _(pe):
            def three(dst, w_h, w_l, m_h, m_l, first, last):
                pe.matmul(dst, w_h, m_h, start=first, stop=False)
                pe.matmul(dst, w_h, m_l, start=False, stop=False)
                return pe.matmul(dst, w_l, m_h, start=False, stop=last)

            def cols(slot, at, n=128):
                return wh[:, slot, at:at + n], wl[:, slot, at:at + n]

            def blocks(dst, slot, mh, ml, n, k0=0, count=KB, first=True, last=True, at=0, ready=None, turn=None):
                for k in range(count):
                    if ready:
                        pe.wait_ge(ready[0], ready[1] + k + 1)
                    if turn is not None and k == count - 1:
                        pe.wait_ge(mod_copied, 2 * turn + 2)
                    if mh is mixh:
                        moving = mh[:, 0:n // SEQ, k, :], ml[:, 0:n // SEQ, k, :]
                    else:
                        moving = mh[:, k0 + k, 0:n], ml[:, k0 + k, 0:n]
                    mm = three(dst, *cols(slot, at + 128 * k), *moving, first and k == 0, last and k == count - 1)
                return mm

            def mod_unit(p, it, j, i):
                v, k = group_of(p, it, i)
                slot = (p.g0 + j) % SLOTS
                if k == 0 and p.mod0 + i:
                    pe.wait_ge(mod_ready, v)
                for half, bank in enumerate(mod_banks(p)):
                    c = slice(half * 512, (half + 1) * 512)
                    passes = [(4, wh[:, slot, c]), (2, wl[:, slot, c])]
                    if k == KB - 1:
                        passes.reverse()
                    for at, (rows, moving) in enumerate(passes):
                        mm = pe.matmul(ps[0:rows, bank, :], silu_split[:, k, 0:rows], moving,
                                       start=k == 0 and at == 0, stop=k == KB - 1 and at == 1)
                mm.then_inc(unit_done, 1)

            def turns(p, it, j):
                i = vector_ends(p, j)
                return None if i is None else group_of(p, it, i)[0]

            def turn_mod(p, it, j):
                v = turns(p, it, j)
                if v is None:
                    return
                if p.name.startswith("mod"):
                    pe.wait_ge(mod_copied, 2 * v + 2)
                for m in range(KB):
                    mm = pe.transpose(ps[:, mod_banks(p)[0], 4 * m:4 * m + 4], mod_rows[0:4, m * 128:(m + 1) * 128], ident[0:4, 0:4])
                mm.then_inc(mod_turned, 1)

            def loop(layer, name, main=None):
                p = PHASES[layer, name]

                def body(it):
                    for j, kind, i in p.places():
                        pe.wait_ge(lo_ready, unit(p, it, j, 1))
                        if kind == "m":
                            mod_unit(p, it, j, i)
                        else:
                            main(p, it, j, i)
                        turn_mod(p, it, j)
                walk(pe, p, body)

            def straight(layer, name):
                p = PHASES[layer, name]
                for j in range(p.units):
                    pe.wait_ge(lo_ready, p.g0 + j + 1)
                    yield j, p, (p.g0 + j) % SLOTS

            def act_bank(p, it, i, per_body):
                pe.wait_ge(act_bank_free, it * per_body + (p.act0 + i + 1))
                return (p.act0 + i) % 2

            def dve_bank(p, it, i, per_body):
                pe.wait_ge(dve_bank_free, it * per_body + (p.dve0 + i + 1))
                return 2 + (p.dve0 + i) % 2

            def rms(v):
                n = NORM_T[v]
                pe.wait_ge(squares_added, added_before(v + 1))
                mm = pe.matmul(ps[:, SUMSQ_BANK[v], 0:n], ones, sq_sum[:, 0:n], start=True, stop=v == 0)
                if v:
                    pe.wait_ge(h_squared, squared_before(v + 1))
                    pe.matmul(ps[:, SUMSQ_BANK[v], 0:n], ones, sq[:, 0, 0:n], start=False, stop=False)
                    pe.wait_ge(last_squared, v)
                    mm = pe.matmul(ps[:, SUMSQ_BANK[v], 0:n], ones, sq[:, 1, 0:n], start=False, stop=True)
                mm.then_inc(sumsq_ready, 1)

            def gates(layer, b):
                n = width(layer)

                def main(p, it, j, i):
                    bank = act_bank(p, it, i, p.mains)
                    blocks(ps[:, bank, 0:n], (p.g0 + j) % SLOTS, xh, xl, n, turn=turns(p, it, j)).then_inc(unit_done, 1)
                loop(layer, "gate_" + b, main)

            pe.wait_ge(sine_in_s, 32)
            pe.matmul(ps[:, 6, 0:SEQ], f_w12[0:HY_EMB, 0, :], emb[0:HY_EMB, :], start=True, stop=True).then_inc(f_pre, 1)
            pe.wait_ge(f_sin, 1)
            pe.matmul(ps[:, 6, 0:SEQ], f_w12[:, 1, :], f_hid[:, :], start=True, stop=True).then_inc(f_pre, 1)

            def filter_taps(f):
                pe.wait_ge(f_sin, 2)
                rows = slice(f * HIDDEN, (f + 1) * HIDDEN)
                for tb in range(2):
                    for d in range(2):
                        mm = pe.matmul(ps[:, 4 + 2 * tb + d, :], f_hid2[rows, tb * 128:(tb + 1) * 128],
                                       f_w3[rows, d * HY:(d + 1) * HY], start=True, stop=True)
                    mm.then_inc(f_taps[f], 1)

            def filter_spectra(f):
                pe.wait_ge(f_abs[f], 2)
                for i in range(4):
                    tb, d = i // 2, i % 2
                    mm = pe.matmul(ps[:, 7, :], ones, envelope[:, tb, d * HY:(d + 1) * HY], start=i == 0, stop=i == 3)
                mm.then_inc(f_l1[f], 1)
                for i, (part, at) in enumerate([(f_even, 0), (f_even, 128), (f_odd, 2 * NFREQ), (f_odd, NFREQ + 128),
                                                (f_even, 2 * NFREQ + 128)]):
                    for tb in range(2):
                        mm = pe.matmul(ps[:, (2, 3, 4, 5, 6)[i], :], ftab0[:, tb, at:at + 128], part[:, tb, :],
                                       start=tb == 0, stop=tb == 1)
                    mm.then_inc(f_spec[f], 1)

            pe.wait_ge(act_bank_free, 2)
            pe.wait_ge(silu_lo, 1)
            pe.wait_ge(consts_in_s, 16)
            for i in range(3):
                loop(0, f"mod{i}")
            pe.wait_ge(f_w3_in_s, 16)
            filter_taps(0)
            rms(0)
            loop(0, "mod3")
            pe.wait_ge(ftab_in_s, 16)
            pe.wait_ge(f_parts[0], 4)
            pe.wait_ge(std_ready, 1)
            filter_spectra(0)
            pe.wait_ge(f_scaled[0], 2)
            for layer in range(DEPTH):
                n = width(layer)
                ns = n // SEQ
                for name in ("q", "kv", "kpe"):
                    if (layer, name) == (0, "kv"):
                        pe.wait_ge(f_scaled[0], 5)
                        filter_taps(1)
                    if (layer, name) == (0, "kpe"):
                        pe.wait_ge(f_parts[1], 4)
                        pe.wait_ge(dve_bank_free, drained(0, "kv"))
                        filter_spectra(1)
                        pe.wait_ge(f_scaled[1], 2)
                    nt = n if name == "q" else T
                    for j, p, slot in straight(layer, name):
                        bank = dve_bank(p, 0, j, 0)
                        if name == "kpe":
                            for k in range(KB):
                                mm = three(ps[0:ROPE, bank, :], *cols(slot, k * ROPE, ROPE), xh[:, k, :], xl[:, k, :], k == 0, k == KB - 1)
                        else:
                            ready = (x_split, 2 * KB * layer) if (name, j) == ("q", 0) else None
                            mm = blocks(ps[:, bank, 0:nt], slot, xh, xl, nt, ready=ready)
                        mm.then_inc(unit_done, 1)
                if layer == 0:
                    pe.wait_ge(f_scaled[1], 5)
                for first, count, bank, nt in ((0, QB, 5, n), (QB, KVB, 6, T)):
                    pe.wait_ge(lat_sq_ready[layer], first + count)
                    for k in range(count):
                        mm = pe.matmul(ps[:, bank, 0:nt], ones, lat_sq[:, first + k, 0:nt], start=k == 0, stop=k == count - 1)
                    mm.then_inc(lat_sumsq[layer], 1)
                for tb in range(T // 128):
                    for k in range(KVB):
                        mm = pe.matmul(ps[:, 7, tb:tb + 1], lat_sq[:, QB + k, tb * 128:(tb + 1) * 128], ones[:, 0:1],
                                       start=k == 0, stop=k == KVB - 1)
                mm.then_inc(lat_sumsq[layer], 1)
                pe.wait_ge(lat_std[layer], 3)
                gates(layer, "c0")
                pe.wait_ge(dve_bank_free, drained(layer, "kpe"))
                pe.matmul(ps[0:ROPE, 6, 0:SEQ], rot[0:ROPE, 0:ROPE], k_pe_raw[0:ROPE, 0:SEQ], start=True, stop=True).then_inc(kpe_rotated[layer], 1)
                for j, p, slot in straight(layer, "uq"):
                    for i in range(2):
                        bank = dve_bank(p, 0, 2 * j + i, 0)
                        blocks(ps[:, bank, 0:n], slot, cqh, cql, n, count=QB, at=i * QL).then_inc((part_done, unit_done)[i], 1)
                    if j == 1:
                        pe.wait_ge(dve_bank_free, drained(layer, "uq", 2))
                        pe.wait_ge(kpe_ready[layer], 1)
                        for b in range(2):
                            mm = pe.matmul(ps[:, 6, b * SEQ:(b + 1) * SEQ], rot, q_pe[:, b, 0:SEQ], start=True, stop=True)
                        mm.then_inc(qpe_rotated[layer], 1)
                for j, p, slot in straight(layer, "ukv"):
                    for i in range(4):
                        bank = dve_bank(p, 0, 4 * j + i, 0)
                        if j == 0:
                            mm = blocks(ps[:, bank, :], slot, ckh, ckl, T, count=KVB, at=i * KVL)
                        else:
                            t = slice(128 * i, 128 * i + 128)
                            for k in range(KVB):
                                w_h, w_l = cols(slot, k * 512, 512)
                                mm = three(ps[:, bank, :], ckh[:, k, t], ckl[:, k, t], w_h, w_l, k == 0, k == KVB - 1)
                        mm.then_inc(unit_done if i == 3 else part_done, 1)
                gates(layer, "c1")

                jobs = [(hd, s) for s in range(ns) for hd in range(HEADS)]

                def scores(jb):
                    hd, s = jobs[jb]
                    k0, keys = (0, T) if s == 0 else (SEQ, CTX)
                    if jb >= 2:
                        pe.wait_ge(exp_done[layer], 2 * (jb - 1))
                    for qb in range(2):
                        q0 = s * SEQ + qb * 128
                        pe.matmul(ps[:, S_BANKS[2 * (jb % 2) + qb], 0:keys], q_t[0:QK, hd, q0:q0 + 128], k_t[0:QK, hd, k0:k0 + keys],
                                  start=True, stop=True).then_inc(scores_ready[layer], 1)

                def transposes(jb):
                    keys = T if jobs[jb][1] == 0 else CTX
                    pe.wait_ge(probs_ready[layer], 2 * jb + 2)
                    if jb:
                        pe.wait_ge(pt_act[layer], jb)
                        pe.wait_ge(pt_dve[layer], min(jb, HEADS))
                    for kb in range(keys // 128):
                        for qb in range(2):
                            at = (kb % 2) * SEQ + qb * 128
                            mm = pe.transpose(ps[:, 6 + kb // 2, at:at + 128], probs[:, 2 * (jb % 2) + qb, kb * 128:(kb + 1) * 128], ident)
                    mm.then_inc(transposed[layer], 1)

                def weighted_values(jb):
                    hd, s = jobs[jb]
                    tb0, nb = (0, 4) if s == 0 else (2, 2)
                    pair = jb // 2
                    if hd % 2 == 0 and pair >= 2:
                        pe.wait_ge(o_ready[layer], pair - 1)
                    pe.wait_ge(pt_act[layer], jb + 1)
                    pe.wait_ge(pt_dve[layer], min(jb + 1, HEADS))
                    rows = slice(64 * (hd % 2), 64 * (hd % 2) + 64)
                    for kb in range(nb):
                        mm = pe.matmul(ps[rows, pair % 2, 0:SEQ], v_t[:, tb0 + kb, hd * VH:(hd + 1) * VH],
                                       probs_t[:, jb % 2, kb, :], start=kb == 0, stop=kb == nb - 1)
                    mm.then_inc(pv_done[layer], 1)

                pe.wait_ge(q_ready[layer], 1)
                if ns == 2:
                    pe.wait_ge(q_ctx_ready, HEADS)
                pe.wait_ge(kpe_spread[layer], HEADS)
                pe.wait_ge(act_bank_free, drained(layer, "gate_c1"))
                if layer:
                    pe.wait_ge(mod_ready, GROUPS)
                pe.wait_ge(dve_bank_free, drained(layer, "ukv"))
                scores(0)
                scores(1)
                for jb in range(len(jobs)):
                    if jb + 2 < len(jobs):
                        scores(jb + 2)
                    transposes(jb)
                    if jb:
                        weighted_values(jb - 1)
                weighted_values(len(jobs) - 1)

                def branch_out(name, ready, before):
                    mh, ml = (mixh, mixl) if name == "hy_out" else (fh, fl)
                    for j, p, slot in straight(layer, name):
                        for i in range(2):
                            bank = dve_bank(p, 0, 2 * j + i, 0)
                            blocks(ps[:, bank, 0:n], slot, mh, ml, n, count=4, at=512 * i,
                                   ready=None if j + i else (ready, before)).then_inc((part_done, unit_done)[i], 1)

                branch_out("wo", o_ready[layer], HEADS // 2 * (ns - 1))
                for j, p, slot in straight(layer, "pool"):
                    bank = act_bank(p, 0, j, 0)
                    blocks(ps[:, bank, 0:n], slot, xh, xl, n).then_inc(unit_done, 1)
                gates(layer, "a0")
                gates(layer, "a1")
                for j, p, slot in straight(layer, "pool_w"):
                    for g in range(4):
                        pe.wait_ge(u_split[layer], g + 1)
                        bank = dve_bank(p, 0, g, 0)
                        three(ps[:, bank, 0:n], *cols(slot, 128 * g), uh[:, g, 0:n], ul[:, g, 0:n], True, True)\
                            .then_inc(unit_done if g == 3 else part_done, 1)
                gates(layer, "a2")
                branch_out("pool_out", dve_bank_free, drained(layer, "pool_w", 0))

                def hy_main(p, it, j, i):
                    bank = dve_bank(p, it, i, p.mains)
                    blocks(ps[:, bank, 0:n], (p.g0 + j) % SLOTS, xh, xl, n).then_inc(unit_done, 1)
                loop(layer, "hy", hy_main)
                pe.wait_ge(zv_ready[layer], HYB)
                for tb in range(2 * ns):
                    if tb >= 2:
                        pe.wait_ge(z_copied[layer], tb - 1)
                    for c in range(HYB):
                        mm = pe.transpose(ps[:, 6 + tb % 2, c * 128:(c + 1) * 128], z[:, c, tb * 128:(tb + 1) * 128], ident)
                    mm.then_inc(z_transposed[layer], 1)
                pe.wait_ge(z_copied[layer], 2 * ns)
                pe.wait_ge(tables_loaded[layer], 48)
                pe.wait_ge(mod_ready, PHASES[layer, "hy"].mod0 // KB)
                pe.wait_ge(dve_bank_free, drained(layer, "hy"))

                def transform(s):
                    if s:
                        pe.wait_ge(spec_tmp_ready[layer], 4 * s)
                        pe.wait_ge(z_cross[layer], 4 * s)
                    for i, at in enumerate((0, 128, NFREQ, NFREQ + 128)):
                        for tb in range(2):
                            mm = pe.matmul(ps[:, 4 + i, :], ftab[:, tb, at:at + 128], z_t[:, 2 * s + tb, :],
                                           start=tb == 0, stop=tb == 1)
                        mm.then_inc(z_spec[layer], 1)

                def inverse(s):
                    pe.wait_ge(spec_ready[layer], 4 * s + 4)
                    if s:
                        pe.wait_ge(hy_mixed[layer], HYB * s)
                    for c in range(HYB):
                        for i in range(4):
                            mm = pe.matmul(ps[:, 2 + c // 2, c % 2 * SEQ:(c % 2 + 1) * SEQ], spec[:, i, c * 128:(c + 1) * 128], itab[:, i, :],
                                           start=i == 0, stop=i == 3)
                        mm.then_inc(conv_done[layer], 1)

                for s, b in enumerate(B_PARTS):
                    if s < ns:
                        transform(s)
                    gates(layer, b)
                    if s < ns:
                        inverse(s)
                pe.wait_ge(hy_mixed[layer], HYB * ns)
                branch_out("hy_out", hy_ready[layer], HYB * (ns - 1))

                def out_main(p, it, j, i):
                    bank = dve_bank(p, it, i, p.mains)
                    blocks(ps[:, bank, 0:n], (p.g0 + j) % SLOTS, xh, xl, n,
                           ready=None if i else (y_split[layer], 0), turn=turns(p, it, j)).then_inc(unit_done, 1)
                loop(layer, "w_out", out_main)
                rms(2 * layer + 1)
                for half in "ab":
                    def up(p, it, j, i):
                        bank = act_bank(p, it, i, p.mains)
                        blocks(ps[:, bank, 0:n], (p.g0 + j) % SLOTS, xh, xl, n,
                               ready=None if i else (x_split, KB * (2 * layer + 1)), turn=turns(p, it, j)).then_inc(unit_done, 1)
                    loop(layer, "ff1" + half, up)

                    def down(p, it, j, i):
                        before = 2 + 16 * (2 * layer + (half == "b")) + 8 * i
                        if i % 2 == 0:
                            bank = dve_bank(p, it, i // 2, p.mains // 2)
                        else:
                            bank = 2 + (p.dve0 + i // 2) % 2
                        blocks(ps[:, bank, 0:n], (p.g0 + j) % SLOTS, hid_h, hid_l, n, k0=8 * (i % 2),
                               first=i % 2 == 0, last=i % 2 == 1, ready=(hid_ready, before) if i < 2 else None,
                               turn=turns(p, it, j)).then_inc(unit_done, 1)
                    loop(layer, "ff2" + half, down)
                rms(2 * layer + 2)




def _units(w):
    def split_k(a, cols):
        k, m = a.shape
        v = a.reshape(k // 128, 128, m // cols, cols).transpose(2, 1, 0, 3)
        return v.reshape(m // cols, 128, k // 128 * cols)

    def padded(a):
        return np.concatenate([a, np.zeros((*a.shape[:2], 1024 - a.shape[2]), a.dtype)], axis=2) if a.shape[2] < 1024 else a

    mod = w["w_mod"].reshape(DEPTH, KB, 128, VECTORS, D).transpose(0, 3, 1, 2, 4).reshape(-1, 128, D)
    out, mod_at = [], 0
    for (layer, name), p in PHASES.items():
        w_in = w["w_in"][layer]

        def columns(at, n):
            return split_k(w_in[:, at:at + n], 128)

        def pairs(a):
            v = split_k(a, 128)
            return v.reshape(4, 2, 128, 512).transpose(0, 2, 1, 3).reshape(4, 128, 1024)

        if name == "q":
            mains = columns(OFF_Q, QL)
        elif name == "kv":
            mains = columns(OFF_KV, KVL)
        elif name == "kpe":
            mains = padded(split_k(w_in[:, OFF_KV + KVL:OFF_GATE], ROPE))
        elif name.startswith("gate_"):
            mains = columns(OFF_GATE + "abc".index(name[5]) * D, D)[GATE_PARTS[name[5:]]:]
        elif name == "uq":
            u = w["w_uq"][layer].reshape(QL, HEADS, QK)
            u = np.concatenate([u[:, :, NOPE:].reshape(QL, -1), u[:, :, :NOPE].reshape(QL, -1)], axis=1)
            v = split_k(u, 128).reshape(3, 2, 128, QL).transpose(0, 2, 1, 3).reshape(3, 128, 2 * QL)
            mains = padded(v)
        elif name == "ukv":
            u = w["w_ukv"][layer].reshape(KVL, HEADS, NOPE + VH)
            k = split_k(u[:, :, :NOPE].reshape(KVL, -1), 128).transpose(1, 0, 2).reshape(1, 128, 1024)
            mains = np.concatenate([k, split_k(u[:, :, NOPE:].reshape(KVL, -1), 512)])
        elif name in ("wo", "pool_out", "hy_out"):
            mains = pairs(w[{"wo": "w_o"}.get(name, name)][layer])
        elif name == "pool":
            mains = columns(0, OFF_HY)
        elif name == "pool_w":
            mains = padded(w["pool_w"][layer].transpose(1, 0, 2).reshape(1, 128, 512))
        elif name == "hy":
            x0, x1, v = (columns(OFF_HY + i * HY, HY) for i in range(3))
            mains = np.concatenate([x1, v, x0])
        elif name == "w_out":
            mains = split_k(w["w_out"][layer], 128)
        elif name.startswith("ff1"):
            mains = split_k(w["w_ff1"][layer], 128)["ab".index(name[-1]) * 16:][:16]
        elif name.startswith("ff2"):
            rows = w["w_ff2"][layer].reshape(2, 2, 1024, D)["ab".index(name[-1])]
            v = np.stack([split_k(r, 128) for r in rows], axis=1)
            mains = v.reshape(16, 128, 1024)
        at = 0
        for kind in p.pattern * p.bodies:
            if kind == "M":
                out.append(mains[at])
                at += 1
            else:
                out.append(mod[mod_at])
                mod_at += 1
    return np.stack(out)


def _params(w):
    def blocks(v):
        v = np.asarray(v)
        return v.reshape(-1, v.shape[-1] // 128, 128).transpose(2, 0, 1).reshape(128, -1)

    def twice(v):
        return np.repeat(v, 2, axis=1)

    def thirds(v):
        return np.concatenate([v[..., HY:2 * HY], v[..., 2 * HY:], v[..., :HY]], axis=-1)

    def hidden(a, b):
        return np.stack([a, b], axis=-1).reshape(DEPTH * HIDDEN, 2)

    c = np.stack([blocks(w["c"][0]), blocks(w["c_ctx"])], axis=2).reshape(128, -1)
    gain = twice(np.concatenate([blocks(w[g][i]) for i in range(DEPTH) for g in ("norm1_g", "norm2_g")], axis=1))
    t = (np.arange(SEQ, dtype=np.float32) / np.float32(SEQ - 1)).reshape(2, 128).T
    not_first = np.ones((128, 2), np.float32)
    not_first[0, 0] = 0
    cols = {"c": c, "gain": gain, "final_g": blocks(w["final_g"]), "pool_scale": blocks(w["pool_scale"]),
            "conv_w": blocks(thirds(w["hy_conv_w"])), "conv_b": blocks(thirds(w["hy_conv_b"])),
            "hy_bias": blocks(w["hy_bias"]), "q_g": blocks(w["q_norm_g"]), "kv_g": blocks(w["kv_norm_g"]),
            "b_mod": twice(blocks(w["b_mod"])), "f_b": hidden(w["hy_f_b1"], w["hy_f_b2"]),
            "f_freq": hidden(w["hy_f_freq1"], w["hy_f_freq2"]), "neg_t": -t, "not_first": not_first,
            "eps": np.full((128, 1), EPS, np.float32)}
    out = np.zeros((128, PARAMS), np.float32)
    for name, (at, n) in _COLS.items():
        out[:, at:at + n] = cols[name]
    return out


def _tables():
    f32 = np.float32
    rot = np.zeros((128, 128), f32)
    q = ROPE // 4
    for m in range(128):
        rot[m + q if m // q % 2 == 0 else m - q, m] = 1
    rows = np.repeat(np.arange(SEQ // GRID_W, dtype=f32), GRID_W)
    cols = np.tile(np.arange(GRID_W, dtype=f32), SEQ // GRID_W)
    half = ROPE // 2
    inv = (f32(10000.0) ** (-np.arange(0, half, 2, dtype=f32) / f32(half))).astype(f32)
    ar, ac = rows[:, None] * inv, cols[:, None] * inv
    angle = np.tile(np.concatenate([ar, ar, ac, ac], axis=1).T, (128 // ROPE, 1)).astype(np.float64)
    sign = np.where(np.arange(128) // q % 2 == 0, -1.0, 1.0)[:, None]
    consts = np.concatenate([np.eye(128), np.ones((128, 128)), rot, np.cos(angle), np.sin(angle) * sign], axis=1).astype(f32)

    n = 2 * SEQ
    t, k = np.arange(SEQ)[:, None], np.arange(NFREQ)[None, :]
    turn = 2 * np.pi * (t * k % n) / n
    c, s = np.cos(turn), -np.sin(turn)
    nyquist = (-1.0) ** np.arange(SEQ)
    s_ny = s.copy()
    s_ny[:, 0] = nyquist
    c_ny = c[:, :128].copy()
    c_ny[:, 0] = nyquist
    fwd = np.concatenate([c, s_ny, s[:, :128], c_ny], axis=1)
    fwd = fwd.reshape(2, 128, FTAB).transpose(1, 0, 2).astype(f32)
    weight = np.where(np.arange(NFREQ) == 0, 1.0, 2.0)[:, None] / n
    inverse = np.concatenate([c.T * weight, s_ny.T * weight])
    inverse = inverse.reshape(4, 128, SEQ).transpose(1, 0, 2).astype(f32)

    at = np.arange(SEQ)
    per = [np.minimum(at + w // 2, SEQ) - np.maximum(at - w // 2, 0) for w in POOL_WINDOWS]
    counts = np.broadcast_to((1.0 / np.stack(per))[None, :, None, :], (128, 4, 2, SEQ)).astype(f32)

    time = np.linspace(0.0, 1.0, SEQ, dtype=f32)[:, None]
    omega = (f32(2.0 * np.pi) * np.arange(SEQ, dtype=f32)[:, None] / f32(SEQ)).astype(f32)
    bands = np.linspace(1e-4, (HY_EMB - 1) // 2 - 1, (HY_EMB - 1) // 2, dtype=f32)[None, :]
    phase = (omega * bands).astype(f32).astype(np.float64)
    emb = np.concatenate([time, np.cos(phase), -np.sin(phase)], axis=1).T.astype(f32)
    return consts, fwd, inverse, counts, emb


def kernel(**inputs):
    import concourse.bacc as bacc
    from concourse.bass_utils import run_bass_kernel_spmd

    w = {k: np.asarray(v) for k, v in inputs.items()}
    consts, fwd, inverse, counts, emb = _tables()
    tokens = np.concatenate([w["x"][0], w["ctx"][0]])
    f_w12 = np.zeros((DEPTH * HIDDEN, 2, DEPTH * HIDDEN), np.float32)
    for i in range(DEPTH):
        own = slice(i * HIDDEN, (i + 1) * HIDDEN)
        f_w12[:HY_EMB, 0, own] = w["hy_f_w1"][i]
        f_w12[own, 1, own] = w["hy_f_w2"][i]
    arrays = {
        "x": tokens.T.reshape(KB, 128, T).transpose(1, 0, 2),
        "units": _units(w),
        "params": _params(w),
        "consts": consts, "fwd": fwd, "inverse": inverse, "counts": counts, "emb": emb,
        "f_w12": f_w12,
        "f_w3": w["hy_f_w3"].reshape(DEPTH * HIDDEN, 2 * HY),
        "decay": w["hy_decay"].reshape(DEPTH, 2 * HY),
    }
    arrays = {f"in_{k}": np.ascontiguousarray(v, np.float32) for k, v in arrays.items()}
    nc = bacc.Bacc("TRN2", target_bir_lowering=False, num_devices=1)
    args = [nc.dram_tensor(k, v.shape, mybir.dt.float32, kind="ExternalInput").ap() for k, v in arrays.items()]
    scratch = nc.dram_tensor("filters", (DEPTH, 128, FILT), mybir.dt.float32, kind="Internal").ap()
    out = nc.dram_tensor("out", (128, KB, SEQ), mybir.dt.float32, kind="ExternalOutput").ap()
    backbone(nc, *args, scratch, out)
    got = run_bass_kernel_spmd(nc, [arrays], core_ids=[0]).results[0]["out"]
    return np.ascontiguousarray(got.transpose(2, 1, 0)).reshape(1, SEQ, D)
```
